# Optimizing a Trainium2 kernel written in Bass

```python
import math
import jax, jax.numpy as jnp
from jax import lax
import numpy as np

D_MODEL = 1024
BATCH = 1
SEQ = 2048
DEPTH = 1

CHUNK = 64
Q_BLOCK = 128

MLA_HEADS = 8
QK_NOPE_DIM = 64
QK_ROPE_DIM = 32
V_HEAD_DIM = 64
Q_LORA_RANK = 256
KV_LORA_RANK = 128
ROPE_THETA = 10000.0
ATTN_WIDTH = MLA_HEADS * V_HEAD_DIM

CONV_GROUPS = 8
CONV_DIM = D_MODEL // 2
CONV_WIDTH = 3

MIX_WIDTH = ATTN_WIDTH + CONV_DIM
IN_SIZES = (Q_LORA_RANK, KV_LORA_RANK, QK_ROPE_DIM, CONV_DIM, CONV_DIM, CONV_DIM)
IN_COLS = sum(IN_SIZES)
IN_OFFSETS = tuple(int(v) for v in np.cumsum(IN_SIZES)[:-1])

N_GROUPS = 4
EXPERTS_PER_GROUP = 8
N_EXPERTS = N_GROUPS * EXPERTS_PER_GROUP
TOP_K = 2
D_EXPERT = 256
DISPATCH_BLOCK = 128

N_MOD = 6
RMS_EPS = 1e-6
NEG_INF = -1e30

kernel_name = 'hymba_mla_shortconv_hmoe_adaln_block'

def rms_norm(x, g):
    xf = x.astype(jnp.float32)
    y = xf * lax.rsqrt(jnp.mean(xf * xf, axis=-1, keepdims=True) + RMS_EPS)
    return (y * g.astype(jnp.float32)).astype(x.dtype)

def modulate(h, shift, scale):
    return h * (1.0 + scale[:, None, :]) + shift[:, None, :]

def rope_tables(positions):
    inv_freq = 1.0 / (ROPE_THETA ** (jnp.arange(0, QK_ROPE_DIM, 2, dtype=jnp.float32) / QK_ROPE_DIM))
    ang = positions.astype(jnp.float32)[..., None] * inv_freq
    return jnp.cos(ang), jnp.sin(ang)

def apply_rope(x, cos, sin):
    xf = x.astype(jnp.float32)
    x1, x2 = xf[..., : QK_ROPE_DIM // 2], xf[..., QK_ROPE_DIM // 2:]
    return jnp.concatenate([x1 * cos - x2 * sin, x2 * cos + x1 * sin], axis=-1).astype(x.dtype)

def mla_mixer(q_c, kv_c, k_r, positions, q_norm_g, kv_norm_g, w_uq, w_uk, w_uv):
    B, S, _ = q_c.shape
    H, DN, DR, DV = MLA_HEADS, QK_NOPE_DIM, QK_ROPE_DIM, V_HEAD_DIM
    q = (rms_norm(q_c, q_norm_g) @ w_uq).reshape(B, S, H, DN + DR)
    q_nope, q_rope = q[..., :DN], q[..., DN:]
    kv = rms_norm(kv_c, kv_norm_g)
    k_nope = (kv @ w_uk).reshape(B, S, H, DN)
    v = (kv @ w_uv).reshape(B, S, H, DV)
    cos, sin = rope_tables(positions)
    q_rope = apply_rope(q_rope, cos[:, :, None, :], sin[:, :, None, :])
    k_rope = apply_rope(k_r, cos, sin)
    nq = S // Q_BLOCK
    qn_b = q_nope.reshape(B, nq, Q_BLOCK, H, DN).transpose(1, 0, 2, 3, 4)
    qr_b = q_rope.reshape(B, nq, Q_BLOCK, H, DR).transpose(1, 0, 2, 3, 4)
    k_chunk = jnp.arange(S) // CHUNK
    sm_scale = 1.0 / math.sqrt(DN + DR)

    def attend_block(args):
        qn, qr, bi = args
        s = (jnp.einsum('bqhd,bkhd->bhqk', qn, k_nope)
             + jnp.einsum('bqhr,bkr->bhqk', qr, k_rope)).astype(jnp.float32) * sm_scale
        q_chunk = (bi * Q_BLOCK + jnp.arange(Q_BLOCK)) // CHUNK
        allowed = k_chunk[None, :] <= q_chunk[:, None]
        s = jnp.where(allowed[None, None], s, NEG_INF)
        p = jax.nn.softmax(s, axis=-1).astype(v.dtype)
        return jnp.einsum('bhqk,bkhd->bqhd', p, v)

    out = lax.map(attend_block, (qn_b, qr_b, jnp.arange(nq)))
    return out.transpose(1, 0, 2, 3, 4).reshape(B, S, ATTN_WIDTH)

def short_conv_mixer(u, b_gate, c_gate, conv_w, conv_b):
    z = c_gate * u
    rhs = conv_w.reshape(CONV_WIDTH, 1, CONV_DIM).astype(z.dtype)
    zc = lax.conv_general_dilated(z, rhs, window_strides=(1,), padding=[(CONV_WIDTH - 1, 0)],
                                  dimension_numbers=('NWC', 'WIO', 'NWC'),
                                  feature_group_count=CONV_DIM)
    return b_gate * (zc + conv_b)

def hier_moe(h, w_rg, b_rg, w_re, b_re, w_gate, w_up, w_down):
    B, S, D = h.shape
    T = B * S
    hf = h.reshape(T, D)
    g_logits = (hf @ w_rg + b_rg).astype(jnp.float32)
    g_prob = jax.nn.softmax(g_logits, axis=-1)
    g_idx = jnp.argmax(g_logits, axis=-1)
    p_group = jnp.take_along_axis(g_prob, g_idx[:, None], axis=1)[:, 0]
    e_logits = (hf @ w_re + b_re).astype(jnp.float32).reshape(T, N_GROUPS, EXPERTS_PER_GROUP)
    e_sel = jnp.take_along_axis(e_logits, g_idx[:, None, None], axis=1)[:, 0]
    top_v, top_i = lax.top_k(e_sel, TOP_K)
    gates = jax.nn.softmax(top_v, axis=-1) * p_group[:, None]
    expert = g_idx[:, None] * EXPERTS_PER_GROUP + top_i
    A = T * TOP_K
    flat_e = expert.reshape(A)
    flat_tok = jnp.repeat(jnp.arange(T, dtype=jnp.int32), TOP_K)
    flat_w = gates.reshape(A)
    order = jnp.argsort(flat_e)
    se, stok, sw = flat_e[order], flat_tok[order], flat_w[order]
    counts = jnp.bincount(flat_e, length=N_EXPERTS)
    starts = jnp.cumsum(counts) - counts
    padded = (counts + DISPATCH_BLOCK - 1) // DISPATCH_BLOCK * DISPATCH_BLOCK
    pend = jnp.cumsum(padded)
    pstarts = pend - padded
    dest = pstarts[se] + (jnp.arange(A) - starts[se])
    n_blocks = -(-A // DISPATCH_BLOCK) + N_EXPERTS
    R = n_blocks * DISPATCH_BLOCK
    buf_tok = jnp.full((R,), T, dtype=jnp.int32).at[dest].set(stok)
    buf_w = jnp.zeros((R,), jnp.float32).at[dest].set(sw)
    blk_e = jnp.minimum(jnp.searchsorted(pend, jnp.arange(n_blocks) * DISPATCH_BLOCK, side='right'),
                        N_EXPERTS - 1)
    h_pad = jnp.concatenate([hf, jnp.zeros((1, D), hf.dtype)], axis=0)

    def expert_block(args):
        tok, e = args
        xb = h_pad[tok]
        a = jax.nn.silu(xb @ w_gate[e]) * (xb @ w_up[e])
        return a @ w_down[e]

    out = lax.map(expert_block, (buf_tok.reshape(n_blocks, DISPATCH_BLOCK), blk_e))
    out = out.reshape(R, D) * buf_w[:, None].astype(out.dtype)
    y = jnp.zeros((T + 1, D), out.dtype).at[buf_tok].add(out)
    return y[:T].reshape(B, S, D)

def setup_inputs(seed: int = 0) -> dict:
    key = jax.random.key(seed)
    ks = jax.random.split(key, 28)
    L, D = DEPTH, D_MODEL
    f32 = jnp.float32

    def nrm(k, shape, scale):
        return jax.random.normal(k, shape, f32) * scale

    def gain(k, shape):
        return 1.0 + 0.02 * jax.random.normal(k, shape, f32)

    offsets = jax.random.randint(ks[2], (BATCH, 1), 0, 4096, dtype=jnp.int32)
    positions = offsets + jnp.arange(SEQ, dtype=jnp.int32)[None, :]
    return {
        'x': jax.random.normal(ks[0], (BATCH, SEQ, D), f32),
        'c': jax.random.normal(ks[1], (BATCH, D), f32),
        'positions': positions,
        'w_ada': nrm(ks[3], (L, D, N_MOD * D), 0.3 * D ** -0.5),
        'b_ada': nrm(ks[4], (L, N_MOD * D), 0.02),
        'norm1_g': gain(ks[5], (L, D)),
        'w_in': nrm(ks[6], (L, D, IN_COLS), D ** -0.5),
        'q_norm_g': gain(ks[7], (L, Q_LORA_RANK)),
        'kv_norm_g': gain(ks[8], (L, KV_LORA_RANK)),
        'w_uq': nrm(ks[9], (L, Q_LORA_RANK, MLA_HEADS * (QK_NOPE_DIM + QK_ROPE_DIM)), Q_LORA_RANK ** -0.5),
        'w_uk': nrm(ks[10], (L, KV_LORA_RANK, MLA_HEADS * QK_NOPE_DIM), KV_LORA_RANK ** -0.5),
        'w_uv': nrm(ks[11], (L, KV_LORA_RANK, MLA_HEADS * V_HEAD_DIM), KV_LORA_RANK ** -0.5),
        'conv_w': nrm(ks[12], (L, CONV_WIDTH, CONV_DIM), CONV_WIDTH ** -0.5),
        'conv_b': nrm(ks[13], (L, CONV_DIM), 0.02),
        'attn_out_g': gain(ks[14], (L, ATTN_WIDTH)),
        'conv_out_g': gain(ks[15], (L, CONV_DIM)),
        'w_out': nrm(ks[16], (L, MIX_WIDTH, D), MIX_WIDTH ** -0.5),
        'norm2_g': gain(ks[17], (L, D)),
        'w_router_group': nrm(ks[18], (L, D, N_GROUPS), D ** -0.5),
        'b_router_group': nrm(ks[19], (L, N_GROUPS), 0.01),
        'w_router_expert': nrm(ks[20], (L, D, N_EXPERTS), D ** -0.5),
        'b_router_expert': nrm(ks[21], (L, N_EXPERTS), 0.01),
        'w_exp_gate': nrm(ks[22], (L, N_EXPERTS, D, D_EXPERT), D ** -0.5),
        'w_exp_up': nrm(ks[23], (L, N_EXPERTS, D, D_EXPERT), D ** -0.5),
        'w_exp_down': nrm(ks[24], (L, N_EXPERTS, D_EXPERT, D), D_EXPERT ** -0.5),
        'final_g': gain(ks[25], (D,)),
    }

def reference(x, c, positions, w_ada, b_ada, norm1_g, w_in, q_norm_g, kv_norm_g, w_uq, w_uk, w_uv,
              conv_w, conv_b, attn_out_g, conv_out_g, w_out, norm2_g, w_router_group, b_router_group,
              w_router_expert, b_router_expert, w_exp_gate, w_exp_up, w_exp_down, final_g):
    c_act = jax.nn.silu(c)
    for l in range(DEPTH):
        mod = c_act @ w_ada[l] + b_ada[l]
        sh1, sc1, g1, sh2, sc2, g2 = jnp.split(mod, N_MOD, axis=-1)
        h = modulate(rms_norm(x, norm1_g[l]), sh1, sc1)
        proj = h @ w_in[l]
        q_c, kv_c, k_r, u, b_gate, c_gate = jnp.split(proj, IN_OFFSETS, axis=-1)
        attn = mla_mixer(q_c, kv_c, k_r, positions, q_norm_g[l], kv_norm_g[l], w_uq[l], w_uk[l], w_uv[l])
        conv = short_conv_mixer(u, b_gate, c_gate, conv_w[l], conv_b[l])
        mixed = jnp.concatenate([rms_norm(attn, attn_out_g[l]), rms_norm(conv, conv_out_g[l])], axis=-1)
        x = x + g1[:, None, :] * (mixed @ w_out[l])
        h2 = modulate(rms_norm(x, norm2_g[l]), sh2, sc2)
        x = x + g2[:, None, :] * hier_moe(h2, w_router_group[l], b_router_group[l], w_router_expert[l],
                                          b_router_expert[l], w_exp_gate[l], w_exp_up[l], w_exp_down[l])
    return rms_norm(x, final_g)


_drawn_inputs = setup_inputs


def setup_inputs(seed=0):
    import zlib

    import numpy as np

    out = dict(_drawn_inputs(seed))
    spreads = {}
    factors = {'norm1_g': 8.0,
     'q_norm_g': 8.0,
     'kv_norm_g': 8.0,
     'conv_b': 38.903,
     'attn_out_g': 8.0,
     'conv_out_g': 8.0,
     'norm2_g': 8.0,
     'b_router_group': 8.0,
     'b_router_expert': 8.0,
     'final_g': 7.792}
    for name, (base, spread) in spreads.items():
        noise = np.random.default_rng([zlib.crc32(name.encode()), seed]).standard_normal(out[name].shape)
        drawn = base * np.exp(spread * noise) if base else spread * noise
        out[name] = __import__('jax').numpy.asarray(drawn.astype(out[name].dtype))
    for name, factor in factors.items():
        out[name] = (out[name] * factor).astype(out[name].dtype)
    return out
```

```python
import math
from contextlib import ExitStack

import numpy as np

import concourse.bass as bass
from concourse import mybir

P = 128
F32 = mybir.dt.float32
F32R = mybir.dt.float32r
BF16 = mybir.dt.bfloat16
I32 = mybir.dt.int32
ALU = mybir.AluOpType
ACT = mybir.ActivationFunctionType
AX = mybir.AxisListType

D = 1024
KD = D // P
S = 2048
NT = S // P
NG = 4
GT = NT // NG
GW = GT * P
HEADS = 8
NOPE = 64
ROPE = 32
QKD = NOPE + ROPE
VD = 64
QR = 256
KQ = QR // P
KVR = 128
ATTN = HEADS * VD
CONV = 512
NCH = CONV // P
TAPS = 3
NEXP = 32
NGRP = 4
EPG = NEXP // NGRP
FE = 256
KF = FE // P
CAP = 192
CAPB = CAP - P
ROUNDS = -(-S // CAP)
EPS = 1e-6
BIG = 1e30
SM = 1.0 / math.sqrt(QKD)

C_ID, C_ONE, C_TRI, C_FOLD = 0, 128, 256, 384
C_FREQ, C_TURN, C_PHASE, C_SIGN, C_PART = 448, 449, 450, 451, 452
C_SLOT, C_EXP, C_GRP, C_RND = 456, 648, 680, 684
C_DUMP = 696
C_ALL = C_DUMP + NEXP

R_BADA, R_N1, R_N2, R_AO, R_CO, R_Q, R_KV, R_CW, R_CB, R_ALL = 0, 48, 56, 64, 68, 72, 74, 75, 87, 91

TWO_PI = 2 * math.pi
PI_1 = 6.28125
PI_2 = math.floor((TWO_PI - PI_1) * 2**19) / 2**19
PI_3 = math.floor((TWO_PI - PI_1 - PI_2) * 2**30) / 2**30
PI_4 = TWO_PI - PI_1 - PI_2 - PI_3
ROUND = 1.5 * 2**23
PI_IN = 3.1415925


def constants():
    c = np.zeros((P, C_ALL), np.float32)
    c[:, C_ID:C_ID + P] = np.eye(P)
    c[:, C_ONE:C_ONE + P] = 1
    c[:, C_TRI:C_TRI + P] = np.triu(np.ones((P, P)), 1)
    i = np.arange(64)
    c[64:, C_FOLD:C_FOLD + 64] = (i[:, None] % ROPE) == (i[None] % ROPE)
    freq = np.float32(1) / (np.float64(10000.0) ** (np.arange(0, ROPE, 2) / ROPE)).astype(np.float32)
    c[64:, C_FREQ] = np.tile(freq, 4)
    c[64:96, C_TURN] = 0.25
    c[64:96, C_PHASE] = math.pi / 2
    c[:, C_SIGN] = 1
    c[96:112, C_SIGN] = -1
    c[:, C_PART] = np.arange(P)
    c[:, C_SLOT:C_SLOT + CAP] = np.arange(CAP)
    c[:, C_EXP:C_EXP + NEXP] = np.arange(NEXP)
    c[:, C_GRP:C_GRP + NGRP] = np.arange(NGRP)
    c[:, C_RND:C_RND + ROUNDS] = np.arange(ROUNDS) * CAP
    c[:, C_DUMP:C_DUMP + NEXP] = 1 + 2 * S + np.arange(P)[:, None] + np.arange(NEXP) % 2 * CAP
    return c


class Steps:

    def __init__(self, eng, sem):
        self.eng, self.sem, self.count, self.last = eng, sem, {}, None
        self.it, self.per, self.base = None, {}, {}

    def __call__(self, ins, sem=None):
        sem = sem or self.sem
        ins.then_inc(sem, 1)
        self.count[sem.name] = self.count.get(sem.name, 0) + 1
        self.last = sem

    def wait(self):
        if self.last is not None:
            n = self.count[self.last.name]
            self.eng.wait_ge(self.last, n if self.it is None else self.it * self.per[self.last.name] + n)

    def enter(self, it, per):
        self.it, self.per, self.base, self.last = it, {s.name: n for s, n in per.items()}, dict(self.count), None

    def leave(self, trips):
        self.wait()
        for k, n in self.count.items():
            made = n - self.base.get(k, 0)
            assert made == self.per.get(k, 0), (k, made)
            self.count[k] = n + made * (trips - 1)
        self.it, self.last = None, None


def hold(eng, sem, value, passed):
    eng.wait_ge(sem, value)
    eng.sem_inc(passed, 1)


def rows(v):
    return v.rearrange("l (r c) -> (l r) c", c=P)


def prepare(nc, T, st):
    with ExitStack() as ctx:
        sb = lambda name, shape, dt=F32: ctx.enter_context(nc.sbuf_tensor(name, shape, dt))
        sem = lambda name: ctx.enter_context(nc.semaphore(name))
        cst, cols, modc, g1row, g2row, fgrow, cs, hT = (st[k] for k in (
            "cst", "cols", "modc", "g1row", "g2row", "fgrow", "cs", "hT"))
        prow = sb("prow", [P, P])
        ccol = sb("ccol", [P, KD])
        csil = sb("csil", [P, KD])
        wada = sb("wada", [P, 2, KD * D])
        acc = sb("acc", [P, 2, D])
        posi = acc[:].rearrange("p a d -> p (a d)").bitcast(I32)
        posf = wada[:, 0, 0:S]
        turns = wada[:, 0, S:2 * S]
        xt = sb("xt", [P, 2, GT, D])
        xsq = sb("xsq", [P, D])
        ss = sb("ss", [P, 2, GT])
        sr = sb("sr", [P, 2, GT])
        rx = sb("rx", [P, 2, GT])
        bank = ctx.enter_context(nc.psum_tensor("pbank", [P, 8, 512], F32))

        ld_small, ld_pos, ld_brow = sem("ld_small"), sem("ld_pos"), sem("ld_brow")
        ld_wada = [sem("ld_wada0"), sem("ld_wada1")]
        ld_x = [sem("ld_x0"), sem("ld_x1")]
        cols_turned, table_done, silu_done = sem("cols_turned"), sem("table_done"), sem("silu_done")
        angle_ready, sines_done = sem("angle_ready"), sem("sines_done")
        acc_ready, acc_used, mod_ready = sem("acc_ready"), sem("acc_used"), sem("mod_ready")
        squares_done, inverse_ready, scale_ready = sem("squares_done"), sem("inverse_ready"), sem("scale_ready")
        x_scaled, turned, h_even, h_odd = sem("x_scaled"), sem("turned"), sem("h_even"), sem("h_odd")
        dve_step, act_step, passed = sem("dve_step0"), sem("act_step0"), sem("passed0")
        block = ctx.enter_context(nc.Block())

        w_ada = T["w_ada"].rearrange("l (p k) n -> p (l k) n", k=KD)
        x_in = T["x"].rearrange("b (g q p) d -> p (b g) q d", p=P, q=GT)

        @block.sync
        def _(sp):
            small = [(cst[:], T["consts"]), (ccol[:], T["c"].rearrange("b (p k) -> p (b k)", k=KD)),
                     (prow[R_BADA:R_N1], rows(T["b_ada"])), (prow[R_N1:R_N2], rows(T["norm1_g"])),
                     (prow[R_N2:R_AO], rows(T["norm2_g"])), (prow[R_AO:R_CO], rows(T["attn_out_g"])),
                     (prow[R_CO:R_Q], rows(T["conv_out_g"])), (prow[R_Q:R_KV], rows(T["q_norm_g"])),
                     (prow[R_KV:R_CW], rows(T["kv_norm_g"])),
                     (prow[R_CW:R_CB], T["conv_w"].rearrange("l t (r c) -> (l t r) c", c=P)),
                     (prow[R_CB:R_ALL], rows(T["conv_b"]))]
            for dst, src in small:
                sp.dma_start(dst, src).then_inc(ld_small, 16)
            sp.dma_start(posi, T["positions"][0:1, :].partition_broadcast(P).rearrange("p a s -> p (a s)")
                         ).then_inc(ld_pos, 16)
            b = T["b_ada"]
            sp.dma_start(g1row[:], b[0, 2 * D:3 * D].partition_broadcast(P)).then_inc(ld_brow, 16)
            sp.dma_start(g2row[:], b[0, 5 * D:6 * D].partition_broadcast(P)).then_inc(ld_brow, 16)
            sp.dma_start(fgrow[:], T["final_g"].partition_broadcast(P)).then_inc(ld_brow, 16)
            for g in range(2):
                sp.dma_start(xt[:, g], x_in[:, g]).then_inc(ld_x[g], 16)
            sp.wait_ge(table_done, 1)
            for j in range(6):
                if j >= 2:
                    sp.wait_ge(acc_ready, j - 1)
                sp.dma_start(wada[:, j % 2].rearrange("p (k n) -> p k n", k=KD),
                             w_ada[:, :, j * D:(j + 1) * D]).then_inc(ld_wada[j % 2], 16)
            for g in range(2, NG):
                sp.wait_ge(turned, KD * (g - 1))
                sp.dma_start(xt[:, g % 2], x_in[:, g]).then_inc(ld_x[g % 2], 16)
            sp.wait_ge(ld_brow, 48)

        @block.vector
        def _(ve):
            V = Steps(ve, dve_step)
            ve.wait_ge(ld_small, 16 * 11)
            ve.wait_ge(ld_pos, 16)
            V(ve.tensor_copy(posf, posi))
            V.wait()
            V(ve.tensor_scalar(posf, posf, cst[:, C_FREQ:C_FREQ + 1], None, ALU.mult))
            V.wait()
            V(ve.tensor_scalar(turns, posf, 1 / TWO_PI, cst[:, C_TURN:C_TURN + 1], ALU.mult, ALU.add))
            V.wait()
            V(ve.tensor_scalar(turns, turns, ROUND, ROUND, ALU.add, ALU.subtract))
            for part in (PI_1, PI_2, PI_3, PI_4):
                V.wait()
                V(ve.scalar_tensor_tensor(posf, turns, -part, posf, ALU.mult, ALU.add))
            V.wait()
            V(ve.tensor_scalar(posf, posf, cst[:, C_PHASE:C_PHASE + 1], PI_IN, ALU.add, ALU.min))
            V.wait()
            V(ve.tensor_scalar(posf, posf, -PI_IN, None, ALU.max), angle_ready)
            ve.wait_ge(sines_done, 1)
            V(ve.tensor_scalar(cs[:], cs[:], cst[:, C_SIGN:C_SIGN + 1], None, ALU.mult))
            V.wait()
            V(ve.memset(cs[0:64, :], 1.0), table_done)
            ve.wait_ge(cols_turned, 1)
            V(ve.tensor_copy(cols[:, 0:R_ALL], bank[:, 0, 0:R_ALL]))
            ve.wait_ge(silu_done, 1)
            for j in range(6):
                a, w = acc[:, j % 2], wada[:, j % 2]
                ve.wait_ge(ld_wada[j % 2], 16 * (j // 2 + 1))
                if j >= 2:
                    ve.wait_ge(acc_used, j - 1)
                V.wait()
                V(ve.tensor_scalar(a, w[:, 0:D], csil[:, 0:1], None, ALU.mult))
                for k in range(1, KD):
                    V.wait()
                    V(ve.scalar_tensor_tensor(a, w[:, k * D:(k + 1) * D], csil[:, k:k + 1], a, ALU.mult, ALU.add),
                      acc_ready if k == KD - 1 else None)
                if j == 1:
                    ve.wait_ge(acc_used, 2)
                    V(ve.tensor_tensor(modc[:, 0:16], bank[:, 1, 0:16], cols[:, 0:16], ALU.add))
                    V.wait()
                    V(ve.scalar_tensor_tensor(modc[:, 8:16], modc[:, 8:16], 1.0, cols[:, R_N1:R_N1 + 8],
                                              ALU.add, ALU.mult), mod_ready)
                if j == 2:
                    ve.wait_ge(acc_used, 3)
                    ve.wait_ge(ld_brow, 48)
                    V(ve.tensor_tensor(g1row[:], g1row[:], bank[:, 2:4].rearrange("p a n -> p (a n)"), ALU.add))
                if j == 4:
                    ve.wait_ge(acc_used, 5)
                    V(ve.tensor_tensor(modc[:, 16:32], bank[:, 1, 16:32], cols[:, 24:40], ALU.add))
                    V.wait()
                    V(ve.scalar_tensor_tensor(modc[:, 24:32], modc[:, 24:32], 1.0, cols[:, R_N2:R_N2 + 8],
                                              ALU.add, ALU.mult))
                if j == 5:
                    ve.wait_ge(acc_used, 6)
                    V(ve.tensor_tensor(g2row[:], g2row[:], bank[:, 2:4].rearrange("p a n -> p (a n)"), ALU.add))
            V.wait()
            with ve.Fori(0, NG // 2) as gp:
                V.enter(gp, {dve_step: 2, inverse_ready: 2, x_scaled: 2 * GT, h_even: KD})
                for b in range(2):
                    ve.wait_ge(squares_done, gp * 2 * GT + b * GT + GT)
                    V.wait()
                    V(ve.tensor_scalar(sr[:, b], ss[:, b], 1 / D, EPS, ALU.mult, ALU.add))
                    V.wait()
                    V(ve.reciprocal(sr[:, b], sr[:, b]), inverse_ready)
                    ve.wait_ge(scale_ready, gp * 2 + b + 1)
                    for q in range(GT):
                        V(ve.tensor_scalar(xt[:, b, q], xt[:, b, q], rx[:, b, q:q + 1], None, ALU.mult), x_scaled)
                    for k in range(0, KD, 2):
                        ve.wait_ge(turned, gp * 2 * KD + b * KD + k + 1)
                        V(ve.tensor_scalar(hT[:, k, bass.ds(gp * 2 * GW + b * GW, GW)], bank[:, 4 + k % 4],
                                           modc[:, 8 + k:9 + k], modc[:, k:k + 1], ALU.mult, ALU.add), h_even)
                V.leave(NG // 2)

        @block.scalar
        def _(act):
            A = Steps(act, act_step)
            act.wait_ge(ld_small, 16 * 11)
            A(act.activation(csil[:], ccol[:], ACT.Silu), silu_done)
            act.wait_ge(angle_ready, 1)
            A(act.activation(cs[:], posf, ACT.Sin), sines_done)
            act.wait_ge(mod_ready, 1)
            A.wait()
            with act.Fori(0, NG // 2) as gp:
                A.enter(gp, {squares_done: 2 * GT, scale_ready: 2, h_odd: KD})
                for b in range(2):
                    hold(act, ld_x[b], gp * 16 + 16, passed)
                    for q in range(GT):
                        A.wait()
                        A(act.activation(xsq[:], xt[:, b, q], ACT.Square, accum_out=ss[:, b, q:q + 1]), squares_done)
                    act.wait_ge(inverse_ready, gp * 2 + b + 1)
                    A(act.activation(rx[:, b], sr[:, b], ACT.Sqrt), scale_ready)
                    for k in range(1, KD, 2):
                        hold(act, turned, gp * 2 * KD + b * KD + k + 1, passed)
                        A(act.activation(hT[:, k, bass.ds(gp * 2 * GW + b * GW, GW)], bank[:, 4 + k % 4],
                                         ACT.Identity, scale=modc[:, 8 + k:9 + k], bias=modc[:, k:k + 1]), h_odd)
                A.leave(NG // 2)

        @block.tensor
        def _(pe):
            pe.wait_ge(ld_small, 16 * 11)
            pe.transpose(bank[:, 0, 0:R_ALL], prow[0:R_ALL, :], cst[0:R_ALL, C_ID:C_ID + R_ALL]
                         ).then_inc(cols_turned, 1)
            for j in range(6):
                pe.wait_ge(acc_ready, j + 1)
                if j in (2, 5):
                    for n in range(2):
                        ins = pe.matmul(bank[:, 2 + n], cst[:, C_ONE:C_ONE + P], acc[:, j % 2, n * 512:(n + 1) * 512],
                                        start=True, stop=True)
                else:
                    at = {0: 0, 1: 8, 3: 16, 4: 24}[j]
                    for k in range(KD):
                        ins = pe.matmul(bank[:, 1, at + k:at + k + 1], acc[:, j % 2, k * P:(k + 1) * P],
                                        cst[:, C_ONE:C_ONE + 1], start=True, stop=True)
                ins.then_inc(acc_used, 1)
            with pe.Fori(0, NG // 2) as gp:
                for b in range(2):
                    pe.wait_ge(x_scaled, gp * 2 * GT + b * GT + GT)
                    for k in range(KD):
                        if k >= 4:
                            pe.wait_ge(h_odd if k % 2 else h_even, gp * KD + b * (KD // 2) + (k - 4) // 2 + 1)
                        elif b:
                            pe.wait_ge(h_odd if k % 2 else h_even, gp * KD + (k + 4) // 2 + 1)
                        else:
                            pe.wait_ge(h_odd if k % 2 else h_even, gp * KD)
                        for q in range(GT):
                            ins = pe.transpose(bank[:, 4 + k % 4, q * P:(q + 1) * P], xt[:, b, q, k * P:(k + 1) * P],
                                               cst[:, C_ID:C_ID + P])
                        ins.then_inc(turned, 1)


KR_COL = QR + KVR
U_COL = KR_COL + ROPE
B_COL = U_COL + CONV
C_COL = B_COL + CONV


def project(nc, T, st):
    with ExitStack() as ctx:
        sb = lambda name, shape, dt=F32: ctx.enter_context(nc.sbuf_tensor(name, shape, dt))
        sem = lambda name: ctx.enter_context(nc.semaphore(name))
        cst, cols, cs, hT, qn, kvn, KR, mix_dram = (st[k] for k in (
            "cst", "cols", "cs", "hT", "qn", "kvn", "KR", "mix_dram"))
        conv = sb("conv", [P, 2, S])
        wsl = sb("wsl", [P, 4, KD, P])
        t1, t2, t3, t4 = sb("t1", [P, S]), sb("t2", [P, S + TAPS - 1]), sb("t3", [P, S]), sb("t4", [P, S])
        bank = ctx.enter_context(nc.psum_tensor("abank", [P, 8, 512], F32))
        half = [bank[:, 0:4].rearrange("p a n -> p (a n)"), bank[:, 4:8].rearrange("p a n -> p (a n)")]

        ld_w = [sem(f"ld_w{i}") for i in range(4)]
        product_done, dve_read, u_copied = sem("product_done"), sem("dve_read"), sem("u_copied")
        squared, inverse_ready, scale_ready = sem("squared"), sem("inverse_ready1"), sem("scale_ready1")
        u_free, conv_stored = sem("u_free"), [sem("conv_stored0"), sem("conv_stored1")]
        dve_step, act_step = sem("dve_step1"), sem("act_step1")
        passed = sem("passed1")
        block = ctx.enter_context(nc.Block())
        w_in = T["w_in"].rearrange("l (k p) n -> p (l k) n", p=P)
        PAIRS = NCH // 2

        @block.sync
        def _(sp):
            for i in range(3):
                sp.dma_start(wsl[:, i], w_in[:, :, i * P:(i + 1) * P]).then_inc(ld_w[i], 16)
            h = ROPE // 2
            sp.dma_start(wsl[:, 3, :, 0:ROPE], w_in[:, :, KR_COL:KR_COL + ROPE]).then_inc(ld_w[3], 16)
            sp.dma_start(wsl[:, 3, :, ROPE:ROPE + h], w_in[:, :, KR_COL + h:KR_COL + ROPE]).then_inc(ld_w[3], 16)
            sp.dma_start(wsl[:, 3, :, ROPE + h:2 * ROPE], w_in[:, :, KR_COL:KR_COL + h]).then_inc(ld_w[3], 16)
            for i, col in enumerate((U_COL, C_COL, B_COL)):
                sp.wait_ge(product_done, i + 1)
                sp.dma_start(wsl[:, i], w_in[:, :, col:col + P]).then_inc(ld_w[i], 16)
            def store(ch, c):
                sp.wait_ge(dve_read, ch * 2 + 9)
                sp.dma_start(mix_dram[:, bass.ds(ch + NCH, 1)], conv[:, c:c + 1]).then_inc(conv_stored[c], 16)

            def weights(ch):
                for i, col in enumerate((U_COL, C_COL, B_COL)):
                    sp.wait_ge(product_done, 7 + ch * 3 - 3 + i + 1)
                    sp.dma_start(wsl[:, i], w_in[:, :, bass.ds(ch * P + col, P)]).then_inc(ld_w[i], 16)

            weights(1)
            with sp.Fori(1, PAIRS) as cp:
                for c in range(2):
                    weights(cp * 2 + c)
                    store(cp * 2 + (c - 2), c)
            store(NCH - 2, 0)
            store(NCH - 1, 1)
            for c in range(2):
                sp.wait_ge(conv_stored[c], 16 * PAIRS)

        @block.tensor
        def _(pe):
            ones = cst[:, C_ONE:C_ONE + P]

            def product(which, slot):
                for k in range(KD):
                    for n in range(4):
                        ins = pe.matmul(bank[:, 4 * which + n], wsl[:, slot, k], hT[:, k, n * 512:(n + 1) * 512],
                                        start=k == 0, stop=k == KD - 1)
                ins.then_inc(product_done, 1)

            def over_partitions(which, parts):
                for n in range(4):
                    for j, part in enumerate(parts):
                        ins = pe.matmul(bank[:, 4 * which + n], ones, part[:, n * 512:(n + 1) * 512],
                                        start=j == 0, stop=j == len(parts) - 1)
                ins.then_inc(product_done, 1)

            pe.wait_ge(ld_w[0], 16)
            product(0, 0)
            pe.wait_ge(ld_w[1], 16)
            product(1, 1)
            pe.wait_ge(ld_w[2], 16)
            pe.wait_ge(dve_read, 1)
            product(0, 2)
            pe.wait_ge(dve_read, 2)
            pe.wait_ge(squared, 2)
            over_partitions(1, (t1, t2))
            pe.wait_ge(ld_w[3], 48)
            pe.wait_ge(dve_read, 3)
            for k in range(KD):
                for n in range(4):
                    ins = pe.matmul(bank[64:128, n], wsl[:, 3, k, 0:64], hT[:, k, n * 512:(n + 1) * 512],
                                    start=k == 0, stop=k == KD - 1)
            ins.then_inc(product_done, 1)
            pe.wait_ge(dve_read, 4)
            pe.wait_ge(squared, 3)
            over_partitions(1, (t3,))
            pe.wait_ge(dve_read, 5)
            for n in range(4):
                ins = pe.matmul(bank[64:128, n], cst[64:128, C_FOLD:C_FOLD + 64], t4[64:128, n * 512:(n + 1) * 512],
                                start=True, stop=True)
            ins.then_inc(product_done, 1)
            with pe.Fori(0, PAIRS) as cp:
                for c in range(2):
                    for i in range(3):
                        pe.wait_ge(ld_w[i], cp * 32 + 16 * c + 32)
                        if i == 2:
                            pe.wait_ge(u_copied, cp * 2 + c + 1)
                        else:
                            pe.wait_ge(dve_read, cp * 4 + 2 * c + 6 + i)
                        product((1 + 3 * c + i) % 2, i)

        @block.vector
        def _(ve):
            V = Steps(ve, dve_step)

            def inverse(which, out, n, count):
                ve.wait_ge(product_done, count)
                V.wait()
                V(ve.tensor_scalar(out, half[which], 1 / n, EPS, ALU.mult, ALU.add), dve_read)
                V.wait()
                V(ve.reciprocal(out, out), inverse_ready)

            ve.wait_ge(product_done, 1)
            V(ve.tensor_copy(qn[:, 0], half[0]), dve_read)
            ve.wait_ge(product_done, 2)
            V(ve.tensor_copy(qn[:, 1], half[1]), dve_read)
            ve.wait_ge(product_done, 3)
            V(ve.tensor_copy(kvn[:], half[0]), dve_read)
            inverse(1, t1[:], QR, 4)
            ve.wait_ge(product_done, 5)
            V(ve.tensor_tensor(t4[64:128], half[0][64:128], cs[64:128], ALU.mult), dve_read)
            ve.wait_ge(scale_ready, 1)
            V(ve.tensor_tensor(qn[:, 0], qn[:, 0], t1[:], ALU.mult))
            V(ve.tensor_tensor(qn[:, 1], qn[:, 1], t1[:], ALU.mult), u_free)
            inverse(1, t3[:], KVR, 6)
            ve.wait_ge(product_done, 7)
            V(ve.tensor_copy(KR[64:128], half[0][64:128]), dve_read)
            ve.wait_ge(scale_ready, 2)
            V(ve.tensor_tensor(kvn[:], kvn[:], t3[:], ALU.mult))
            V(ve.memset(t2[:, 0:TAPS - 1], 0.0))
            V.wait()
            with ve.Fori(0, PAIRS) as cp:
                V.enter(cp, {dve_step: 2 * TAPS, dve_read: 4})
                for c in range(2):
                    tap = lambda i: cols[:, bass.ds(cp * 2 + (c + R_CW + i * NCH), 1)]
                    ve.wait_ge(product_done, cp * 6 + 3 * c + 7 + 2)
                    ve.wait_ge(u_copied, cp * 2 + c + 1)
                    V(ve.tensor_tensor(t2[:, TAPS - 1:], half[(1 + 3 * c + 1) % 2], t1[:], ALU.mult), dve_read)
                    V.wait()
                    V(ve.tensor_scalar(t3[:], t2[:, 2:], tap(2), cols[:, bass.ds(cp * 2 + (c + R_CB), 1)],
                                       ALU.mult, ALU.add))
                    for i in (1, 0):
                        V.wait()
                        V(ve.scalar_tensor_tensor(t3[:], t2[:, i:i + S], tap(i), t3[:], ALU.mult, ALU.add))
                    ve.wait_ge(product_done, cp * 6 + 3 * c + 7 + 3)
                    V.wait()
                    ve.wait_ge(conv_stored[c], cp * 16)
                    V(ve.tensor_tensor(conv[:, c], half[(1 + 3 * c + 2) % 2], t3[:], ALU.mult), dve_read)
                V.leave(PAIRS)

        @block.scalar
        def _(act):
            A = Steps(act, act_step)
            act.wait_ge(dve_read, 1)
            A(act.activation(t1[:], qn[:, 0], ACT.Square), squared)
            act.wait_ge(dve_read, 2)
            A(act.activation(t2[:, 0:S], qn[:, 1], ACT.Square), squared)
            act.wait_ge(dve_read, 3)
            A(act.activation(t3[:], kvn[:], ACT.Square), squared)
            act.wait_ge(inverse_ready, 1)
            A(act.activation(t1[:], t1[:], ACT.Sqrt), scale_ready)
            act.wait_ge(inverse_ready, 2)
            A(act.activation(t3[:], t3[:], ACT.Sqrt), scale_ready)
            A.wait()
            with act.Fori(0, PAIRS) as cp:
                A.enter(cp, {u_copied: 2})
                for c in range(2):
                    act.wait_ge(product_done, cp * 6 + 3 * c + 7 + 1)
                    act.wait_ge(dve_read, cp * 4 + 2 * c + 7)
                    A.wait()
                    A(act.activation(t1[:], half[(1 + 3 * c) % 2], ACT.Copy), u_copied)
                A.leave(PAIRS)


GQ = 4
GROUPS = NT // GQ
STEP_OF = [(g, kt) for g in range(GROUPS) for kt in range(GQ * (g + 1))]
STEPS_HEAD = len(STEP_OF)
CHUNK_OF = [(i, n) for i in range(NT) for n in range(i // GQ + 1)]
assert len(CHUNK_OF) == STEPS_HEAD
AHEAD = 20
TILE_END = [CHUNK_OF.index((i, i // GQ)) for i in range(NT)]
SPREAD = [TILE_END[GQ * (g + 1) - 1] + 2 - AHEAD for g in range(GROUPS)]
SPREAD_AT = {m % STEPS_HEAD: (g, m < 0) for g, m in enumerate(SPREAD)}
MAXIMA_AHEAD = sum(c < AHEAD for c in TILE_END)
GROUPS_AHEAD = sum(m < 0 for m in SPREAD)
PART_AT = {2 + 2 * c: c for c in range(8)}
V_PARTS = NT // 4
V_AT = [(1, STEPS_HEAD - NT + 4 * (v + 1)) if v < V_PARTS - 1 else (0, 1) for v in range(V_PARTS)]
V_EARLY = V_PARTS - 1


def attend(nc, T, st):
    with ExitStack() as ctx:
        sb = lambda name, shape, dt=F32: ctx.enter_context(nc.sbuf_tensor(name, shape, dt))
        sem = lambda name: ctx.enter_context(nc.semaphore(name))
        cst, cols, cs, qn, kvn, KR, mix_dram = (st[k] for k in (
            "cst", "cols", "cs", "qn", "kvn", "KR", "mix_dram"))
        Qhi, Qlo = sb("Qhi", [P, 2, S], F32R), sb("Qlo", [P, 2, S], F32R)
        Khi, Klo = sb("Khi", [P, 2, S], F32R), sb("Klo", [P, 2, S], F32R)
        VV = sb("VV", [P, NT, 3 * VD])
        probs = sb("probs", [P, 3, 512])
        qf, turned_q = sb("qf", [P, 2, 512]), sb("turned_q", [P, 512])
        diag, onesr = sb("diag", [P, 2, 512], F32R), sb("onesr", [P, P], F32R)
        identr, hide, hidef = sb("identr", [64, 64], F32R), sb("hide", [64, P], F32R), sb("hidef", [64, P])
        rs, on = sb("rs", [P, 512]), sb("on", [P, 2, 512])
        wuq = sb("wuq", [P, KQ, (HEADS + 1) * QKD])
        wuk, wuv = sb("wuk", [P, (HEADS + 1) * NOPE]), sb("wuv", [P, (HEADS + 2) * VD])
        wq, wk = sb("wq", [P, 2, KQ, P]), sb("wk", [P, 2, NOPE])
        cmax, nmax = sb("cmax", [P, 2, 4]), sb("nmax", [P, NT])
        bank = ctx.enter_context(nc.psum_tensor("tbank", [P, 8, 512], F32))
        scores, plain, outp, made, spread = bank[:, 0:2], bank[:, 2:4], bank[:, 4:6], bank[:, 6], bank[:, 7]

        ld_up = sem("ld_up")
        weights_ready, made_done, vmade_done, made_dve, v_copied = (sem(n) for n in (
            "weights_ready", "made_done", "vmade_done", "made_dve", "v_copied"))
        khi_done, qf_ready, qhi_done, qlo_done = (sem(n) for n in ("khi_done", "qf_ready", "qhi_done", "qlo_done"))
        plain_done, plain_read, max_ready, diag_ready, spread_done, neg_copied = (sem(n) for n in (
            "plain_done", "plain_read", "max_ready", "diag_ready", "spread_done", "neg_copied"))
        scores_done, exp_done, out_done, out_free = (sem(n) for n in (
            "scores_done", "exp_done", "out_done", "out_free"))
        stored = [sem("on_stored0"), sem("on_stored1")]
        dve_step, act_step, passed_pool = sem("dve_step2"), sem("act_step2"), sem("passed_pool2")
        block = ctx.enter_context(nc.Block())

        def key_cols(i, n):
            return min(512, (i + 1) * P - n * 512)

        def first_tile(g, kt):
            return max(kt - GQ * g, 0)

        def chunk_at(m):
            return (m + AHEAD) % STEPS_HEAD, m + AHEAD >= STEPS_HEAD

        def maxima_before(m):
            return sum(chunk_at(k)[0] in TILE_END for k in range(m))

        @block.sync
        def _(sp):
            q = T["w_uq"].rearrange("l (k p) n -> p (l k) n", p=P)
            sp.dma_start(wuq[:, :, 0:HEADS * QKD], q).then_inc(ld_up, 16)
            sp.dma_start(wuq[:, :, HEADS * QKD:], q[:, :, 0:QKD]).then_inc(ld_up, 16)
            for w, name, more in ((wuk, "w_uk", 1), (wuv, "w_uv", 2)):
                src = T[name].rearrange("l p n -> p (l n)")
                sp.dma_start(w[:, 0:HEADS * NOPE], src).then_inc(ld_up, 16)
                sp.dma_start(w[:, HEADS * NOPE:], src[:, 0:more * NOPE]).then_inc(ld_up, 16)
            sp.sem_inc(stored[0], 16)
            with sp.Fori(0, HEADS // 2) as hp:
                for b in range(2):
                    at = slice(64 * b, 64 * b + 64)
                    for g in range(GROUPS):
                        sp.wait_ge(out_free, hp * 2 * GROUPS + (b * GROUPS + g + 2))
                        sp.dma_start(mix_dram[at, bass.ds(hp, 1), g * 512:(g + 1) * 512],
                                     on[at, (g + 1) % 2:(g + 1) % 2 + 1]).then_inc(stored[(g + 1) % 2], 16)
            sp.wait_ge(stored[0], 16 * (HEADS * GROUPS // 2 + 1))
            sp.wait_ge(stored[1], 16 * HEADS * GROUPS // 2)

        @block.tensor
        def _(pe):
            def make(c, b):
                n = c // 2
                if c % 2 == 0:
                    ins = pe.matmul(made[0:NOPE], wk[:, b], kvn[:, n * 512:(n + 1) * 512], start=True, stop=True)
                else:
                    for k in range(KQ):
                        ins = pe.matmul(made, wq[:, b, k], qn[:, k, n * 512:(n + 1) * 512],
                                        start=k == 0, stop=k == KQ - 1)
                ins.then_inc(made_done, 1)

            def make_values(v, pair):
                for j in range(4):
                    t = v * 4 + j
                    ins = pe.matmul(made[:, j * P:(j + 1) * P], kvn[:, t * P:(t + 1) * P],
                                    wuv[:, bass.ds(pair * 2 * VD, 2 * VD)], start=True, stop=True)
                ins.then_inc(vmade_done, 1)

            def plain_scores(chunk, b, seq):
                i, n = CHUNK_OF[chunk]
                w = key_cols(i, n)
                if not (isinstance(seq, int) and seq < 2):
                    pe.wait_ge(plain_read, seq - 1)
                pe.matmul(plain[:, chunk % 2, 0:w], Qhi[0:QKD, b, i * P:(i + 1) * P],
                          Khi[0:QKD, b, n * 512:n * 512 + w], start=True, stop=True).then_inc(plain_done, 1)

            def spread_maxima(g, head):
                pe.wait_ge(diag_ready, head * NT + GQ * (g + 1))
                if not (isinstance(head, int) and g == 0):
                    pe.wait_ge(neg_copied, head * GROUPS + g)
                pe.matmul(spread, onesr[:], diag[:, g % 2], start=True, stop=True).then_inc(spread_done, 1)

            pe.wait_ge(weights_ready, 1)
            for c in range(8):
                if c:
                    pe.wait_ge(made_dve, c)
                make(c, 0)
            pe.wait_ge(made_dve, 8)
            for v in range(V_EARLY):
                if v:
                    pe.wait_ge(v_copied, v)
                make_values(v, 0)
            pe.wait_ge(qlo_done, 4)
            for chunk in range(AHEAD):
                plain_scores(chunk, 0, chunk)
                if chunk - AHEAD in SPREAD:
                    spread_maxima(SPREAD.index(chunk - AHEAD), 0)
            with pe.Fori(0, HEADS // 2) as hp:
                for b in range(2):
                    head = hp * 2 + b
                    nxt = hp * 2 + (b + 1)

                    def score(m):
                        g, kt = STEP_OF[m]
                        j = first_tile(g, kt)
                        out = scores[:, m % 2, j * P:512]
                        q = slice(g * 512 + j * P, (g + 1) * 512)
                        k = slice(kt * P, (kt + 1) * P)
                        if kt == 0:
                            pe.wait_ge(neg_copied, head * GROUPS + (g + 1))
                        pe.matmul(out, Khi[0:QKD + 1, b, k], Qhi[0:QKD + 1, b, q], start=True, stop=False)
                        pe.matmul(out, Klo[0:QKD + 1, b, k], Qhi[0:QKD + 1, b, q], start=False, stop=False)
                        ins = pe.matmul(out, Khi[0:QKD + 1, b, k], Qlo[0:QKD + 1, b, q], start=False,
                                        stop=kt < GQ * g)
                        if kt >= GQ * g:
                            ins = pe.matmul(scores[:, m % 2, j * P:j * P + 64], hide[:], identr[:],
                                            start=False, stop=True)
                        ins.then_inc(scores_done, 1)

                    def value(m):
                        g, kt = STEP_OF[m]
                        pe.wait_ge(exp_done, hp * 2 * STEPS_HEAD + (b * STEPS_HEAD + m + 1))
                        if kt == 0:
                            pe.wait_ge(out_free, head * GROUPS + g)
                        if b == 0 and (g, kt) == (GROUPS - 1, 4 * V_EARLY):
                            pe.wait_ge(v_copied, hp * V_PARTS + V_PARTS)
                        j = first_tile(g, kt)
                        ins = pe.matmul(outp[:, g % 2, j * P:512], VV[:, kt, b * VD:(b + 2) * VD],
                                        probs[:, m % 3, j * P:512], start=kt == 0, stop=kt == GQ * (g + 1) - 1)
                        if kt == GQ * (g + 1) - 1:
                            ins.then_inc(out_done, 1)

                    if b == 0:
                        pe.wait_ge(v_copied, hp * V_PARTS + V_EARLY)
                    score(0)
                    for m in range(STEPS_HEAD):
                        if m + 1 < STEPS_HEAD:
                            score(m + 1)
                        chunk, ahead = chunk_at(m)
                        if chunk == 0:
                            pe.wait_ge(qlo_done, nxt * 4 + 4)
                        plain_scores(chunk, 1 - b if ahead else b, hp * 2 * STEPS_HEAD + (b * STEPS_HEAD + AHEAD + m))
                        if m in PART_AT:
                            c = PART_AT[m]
                            if c == 0:
                                pe.wait_ge(weights_ready, nxt + 1)
                                if b == 0:
                                    pe.wait_ge(v_copied, hp * V_PARTS + V_PARTS)
                                else:
                                    pe.wait_ge(made_dve, nxt * 8)
                            else:
                                pe.wait_ge(made_dve, nxt * 8 + c)
                            make(c, 1 - b)
                        if (b, m) in V_AT:
                            v = V_AT.index((b, m))
                            if v == 0:
                                pe.wait_ge(made_dve, nxt * 8 + 8)
                            else:
                                pe.wait_ge(v_copied, hp * V_PARTS + (v if b == 0 else V_PARTS + v))
                            make_values(v, hp + b)
                        value(m)
                        if m in SPREAD_AT:
                            g, ahead = SPREAD_AT[m]
                            spread_maxima(g, nxt if ahead else head)

        @block.vector
        def _(ve):
            W = Steps(ve, dve_step)

            def weights(b, head):
                h = ROPE // 2
                at = head * QKD
                W(ve.tensor_copy(wq[:, b, :, 0:QKD], wuq[:, :, bass.ds(at, QKD)]))
                W(ve.tensor_copy(wq[:, b, :, QKD:QKD + h], wuq[:, :, bass.ds(at + (NOPE + h), h)]))
                W(ve.tensor_copy(wq[:, b, :, QKD + h:P], wuq[:, :, bass.ds(at + NOPE, h)]))
                W(ve.tensor_copy(wk[:, b], wuk[:, bass.ds(head * NOPE, NOPE)]), weights_ready)

            def part(c, b, head):
                n = c // 2
                at = slice(n * 512, (n + 1) * 512)
                if c % 2 == 0:
                    ve.wait_ge(khi_done, head * 4 + (n + 1))
                    W(ve.tensor_tensor(Klo[0:NOPE, b, at], made[0:NOPE], Khi[0:NOPE, b, at].bitcast(F32),
                                       ALU.subtract), made_dve)
                else:
                    ve.wait_ge(made_done, head * 8 + (c + 1))
                    ve.wait_ge(qlo_done, head * 4 + max(n - 1, 0))
                    W.wait()
                    W(ve.tensor_tensor(qf[0:QKD, n % 2], made[0:QKD], cs[0:QKD, at], ALU.mult))
                    W(ve.tensor_tensor(turned_q[NOPE:QKD], made[QKD:P], cs[QKD:P, at], ALU.mult), made_dve)
                    W.wait()
                    W(ve.tensor_tensor(qf[NOPE:QKD, n % 2], qf[NOPE:QKD, n % 2], turned_q[NOPE:QKD], ALU.add),
                      qf_ready)

            def maximum(chunk, seq):
                i, n = CHUNK_OF[chunk]
                last = chunk == TILE_END[i]
                w = key_cols(i, n)
                ve.wait_ge(plain_done, seq + 1)
                if last:
                    W(ve.memset(plain[0:64, chunk % 2, w - 64:w], -BIG))
                    W.wait()
                W(ve.tensor_reduce(cmax[:, i % 2, n:n + 1], plain[:, chunk % 2, 0:w], AX.X, ALU.max), plain_read)
                if last:
                    W.wait()
                    W(ve.tensor_reduce(nmax[:, i:i + 1], cmax[:, i % 2, 0:n + 1], AX.X, ALU.max, negate=True),
                      max_ready)

            def divide(r, g, b, head):
                own = slice(64 * b, 64 * b + 64)
                sums = slice(64 - 64 * b, 128 - 64 * b)
                if r == 0:
                    ve.wait_ge(out_done, head * GROUPS + (g + 1))
                W(ve.reciprocal(rs[own, r * P:(r + 1) * P], outp[sums, g % 2, r * P:(r + 1) * P]))
                if r == 3:
                    p = (g + 1) % 2
                    ve.wait_ge(stored[p], (head * 2 + (g + 1) // 2) * 16)
                    W.wait()
                    W(ve.tensor_tensor(on[own, p], outp[own, g % 2], rs[own], ALU.mult), out_free)

            ve.wait_ge(ld_up, 16 * 6)
            for k in range(KQ):
                W(ve.tensor_scalar(wuq[:, k], wuq[:, k], cols[:, R_Q + k:R_Q + k + 1], SM, ALU.mult, ALU.mult))
            W(ve.tensor_scalar(wuk[:], wuk[:], cols[:, R_KV:R_KV + 1], None, ALU.mult))
            W(ve.tensor_scalar(wuv[:], wuv[:], cols[:, R_KV:R_KV + 1], None, ALU.mult))
            W.wait()
            weights(0, 0)
            W(ve.memset(VV[:, :, VD:2 * VD], 1.0))
            W(ve.memset(outp[:, 1], 1.0))
            W(ve.tensor_copy(identr[:], cst[0:64, C_ID:C_ID + 64]))
            W(ve.tensor_copy(onesr[:], cst[:, C_ONE:C_ONE + P]))
            W(ve.memset(hidef[:, 0:64], 0.0))
            W(ve.memset(hidef[:, 64:P], -BIG))
            W.wait()
            W(ve.tensor_copy(hide[:], hidef[:]))
            one = cst[QKD:QKD + 1, C_ONE:C_ONE + 1].to_broadcast([1, S])
            for b in range(2):
                W(ve.tensor_copy(Khi[QKD:QKD + 1, b], one))
                W(ve.tensor_scalar(Klo[QKD:QKD + 1, b], one, 0.0, None, ALU.mult))
                W(ve.tensor_scalar(Qlo[QKD:QKD + 1, b], one, 0.0, None, ALU.mult))
                W(ve.tensor_copy(Khi[NOPE:QKD, b], KR[NOPE:QKD]))
                W.wait()
                W(ve.tensor_tensor(Klo[NOPE:QKD, b], KR[NOPE:QKD], Khi[NOPE:QKD, b].bitcast(F32), ALU.subtract))
            for c in range(8):
                part(c, 0, 0)
            W.wait()
            for chunk in range(AHEAD):
                maximum(chunk, chunk)
            W.wait()
            with ve.Fori(0, HEADS // 2) as hp:
                W.enter(hp, {dve_step: 2 * (3 + 4 + NT + GROUPS * 4), weights_ready: 2, made_dve: 16, qf_ready: 8,
                             plain_read: 2 * STEPS_HEAD, max_ready: 2 * NT, out_free: 2 * GROUPS})
                for b in range(2):
                    for m in range(STEPS_HEAD):
                        g, kt = STEP_OF[m]
                        maximum(chunk_at(m)[0], hp * 2 * STEPS_HEAD + (b * STEPS_HEAD + AHEAD + m))
                        if m == 0:
                            W.wait()
                            weights(1 - b, hp * 2 + (b + 1))
                        if m in PART_AT:
                            part(PART_AT[m], 1 - b, hp * 2 + (b + 1))
                        if kt < 4:
                            if g:
                                divide(kt, g - 1, b, hp * 2 + b)
                            else:
                                divide(kt, GROUPS - 1, 1 - b, hp * 2 + (b - 1))
                    if b == 0:
                        W.wait()
                W.leave(HEADS // 2)
            for r in range(4):
                divide(r, GROUPS - 1, 1, HEADS - 1)

        @block.scalar
        def _(act):
            A = Steps(act, act_step)

            def part(c, b, head):
                n = c // 2
                at = slice(n * 512, (n + 1) * 512)
                if c % 2 == 0:
                    act.wait_ge(made_done, head * 8 + (c + 1))
                    A(act.activation(Khi[0:NOPE, b, at], made[0:NOPE], ACT.Copy), khi_done)
                else:
                    act.wait_ge(qf_ready, head * 4 + (n + 1))
                    A(act.activation(Qhi[0:QKD, b, at], qf[0:QKD, n % 2], ACT.Copy), qhi_done)

            def copy_values(v, pair):
                act.wait_ge(vmade_done, pair * V_PARTS + (v + 1))
                A(act.activation(VV[:, v * 4:(v + 1) * 4].rearrange("p t (c d) -> p t c d", d=VD)[:, :, 0::2],
                                 made.rearrange("p (t c d) -> p t c d", c=2, d=VD), ACT.Copy), v_copied)

            def copy_maxima(g, b, head):
                act.wait_ge(spread_done, head * GROUPS + (g + 1))
                A(act.activation(Qhi[QKD:QKD + 1, b, g * 512:(g + 1) * 512], spread[QKD:QKD + 1], ACT.Copy),
                  neg_copied)

            for c in range(8):
                part(c, 0, 0)
            for v in range(V_EARLY):
                copy_values(v, 0)
            for g in range(GROUPS_AHEAD):
                copy_maxima(g, 0, 0)
            with act.Fori(0, HEADS // 2) as hp:
                for b in range(2):
                    for m in range(STEPS_HEAD):
                        g, kt = STEP_OF[m]
                        j = first_tile(g, kt)
                        act.wait_ge(scores_done, hp * 2 * STEPS_HEAD + (b * STEPS_HEAD + m + 1))
                        A(act.activation(probs[:, m % 3, j * P:512], scores[:, m % 2, j * P:512], ACT.Exp), exp_done)
                        if m in PART_AT:
                            part(PART_AT[m], 1 - b, hp * 2 + (b + 1))
                        if (b, m) in V_AT:
                            copy_values(V_AT.index((b, m)), hp + b)
                        if m in SPREAD_AT:
                            g, ahead = SPREAD_AT[m]
                            copy_maxima(g, 1 - b if ahead else b, hp * 2 + (b + ahead))

        @block.gpsimd
        def _(po):
            def rest(n, b, head):
                at = slice(n * 512, (n + 1) * 512)
                hold(po, qhi_done, head * 4 + (n + 1), passed_pool)
                po.tensor_tensor(Qlo[0:QKD, b, at], qf[0:QKD, n % 2], Qhi[0:QKD, b, at].bitcast(F32), ALU.subtract
                                 ).then_inc(qlo_done, 1)

            def diagonal(i, head):
                hold(po, max_ready, head * NT + (i + 1), passed_pool)
                po.tensor_scalar(diag[:, i // GQ % 2, i % GQ * P:(i % GQ + 1) * P], cst[:, C_ID:C_ID + P],
                                 nmax[:, i:i + 1], None, ALU.mult).then_inc(diag_ready, 1)

            for n in range(4):
                rest(n, 0, 0)
            for i in range(MAXIMA_AHEAD):
                diagonal(i, 0)
            with po.Fori(0, HEADS // 2) as hp:
                for b in range(2):
                    for m in range(STEPS_HEAD):
                        chunk, ahead = chunk_at(m)
                        if chunk in TILE_END:
                            diagonal(TILE_END.index(chunk), hp * 2 + (b + ahead))
                        if PART_AT.get(m, 0) % 2:
                            rest(PART_AT[m] // 2, 1 - b, hp * 2 + (b + 1))


def mix(nc, T, st):
    with ExitStack() as ctx:
        sb = lambda name, shape, dt=F32: ctx.enter_context(nc.sbuf_tensor(name, shape, dt))
        sem = lambda name: ctx.enter_context(nc.semaphore(name))
        cst, cols, modc, g1row, logits, mix_dram, x2_dram, xs_dram = (st[k] for k in (
            "cst", "cols", "modc", "g1row", "logits", "mix_dram", "x2_dram", "xs_dram"))
        NR = NGRP + NEXP
        wout = sb("wout", [P, 2 * NCH, D])
        whi, wlo = sb("whi", [P, 2 * NCH, D], F32R), sb("wlo", [P, 2 * NCH, D], F32R)
        mhi, mlo = sb("mhi", [P, 2, 2 * NCH, P], F32R), sb("mlo", [P, 2, 2 * NCH, P], F32R)
        wr, wrs = sb("wr", [P, KD, NR]), sb("wrs", [P, KD, NR])
        shift = sb("shift", [P, KD, P])
        rbias = sb("rbias", [P, NR])
        xin, mixed = sb("xin", [P, 2, D]), sb("mixed", [P, 2, 2 * NCH, P])
        sq, sqs = sb("sq", [P, 2 * NCH, P]), sb("sqs", [P, 2, P])
        junk = sb("junk", [P, D])
        x2, xs, xT = sb("x2", [P, 2, D]), sb("xs", [P, 2, D]), sb("xT", [P, 2, KD, P])
        mstat, xstat = sb("mstat", [P, 2, 2, 2]), sb("xstat", [P, 2, 3])
        bank = ctx.enter_context(nc.psum_tensor("mbank", [P, 8, 512], F32))
        sums, logit_bank, turn = bank[:, 0, 0:2], bank[:, 1, 0:NR], bank[:, 2:4]
        product = [bank[:, 4:6], bank[:, 6:8]]

        ld_wout, ld_r = sem("ld_wout"), sem("ld_r")
        ld_xin, ld_mixed = [sem("ld_xin0"), sem("ld_xin1")], [sem("ld_mixed0"), sem("ld_mixed1")]
        st_x2, st_xs = [sem("st_x20"), sem("st_x21")], [sem("st_xs0"), sem("st_xs1")]
        folded, whi_ready, wlo_ready = sem("folded"), sem("whi_ready"), sem("wlo_ready")
        shift_ready, rbias_done = sem("shift_ready"), sem("rbias_done")
        m_squared, m_reduced, m_summed, m_mean, m_inverse, m_scale = (sem(n) for n in (
            "m_squared", "m_reduced", "m_summed", "m_mean", "m_inverse", "m_scale"))
        mhi_ready, mlo_ready = sem("mhi_ready"), sem("mlo_ready")
        attn_done, conv_done, attn_added, x2_ready, x2_squared, mean_x, x2_inverse, x2_scale, xs_ready = (
            sem(n) for n in ("attn_done", "conv_done", "attn_added", "x2_ready", "x2_squared", "mean_x",
                             "x2_inverse", "x2_scale", "xs_ready"))
        x_turned, x_copied, routed, logit_ready = (sem(n) for n in ("x_turned", "x_copied", "routed", "logit_ready"))
        passed, passed_pool = sem("passed3"), sem("passed_pool3")
        block = ctx.enter_context(nc.Block())
        x_rows = T["x"].rearrange("b s d -> (b s) d")

        def tiles(eng, step):
            step(0, 0)
            step(1, 1)
            with eng.Fori(0, (NT - 4) // 2) as i:
                for b in range(2):
                    step(i * 2 + (2 + b), b)
            step(NT - 2, 0)
            step(NT - 1, 1)

        def uses(t, b):
            return t // 2 * 16 if isinstance(t, int) else (t - b) * 8

        @block.sync
        def _(sp):
            sp.dma_start(wout[:], T["w_out"].rearrange("l (k p) n -> p (l k) n", p=P)).then_inc(ld_wout, 16)
            sp.dma_start(wr[:, :, 0:NGRP], T["w_router_group"].rearrange("l (k p) n -> p (l k) n", p=P)
                         ).then_inc(ld_r, 16)
            sp.dma_start(wr[:, :, NGRP:], T["w_router_expert"].rearrange("l (k p) n -> p (l k) n", p=P)
                         ).then_inc(ld_r, 16)
            sp.dma_start(rbias[:, 0:NGRP], T["b_router_group"][0, :].partition_broadcast(P)).then_inc(ld_r, 16)
            sp.dma_start(rbias[:, NGRP:], T["b_router_expert"][0, :].partition_broadcast(P)).then_inc(ld_r, 16)

            def load(t, b):
                sp.dma_start(mixed[:, b], mix_dram[:, :, bass.ds(t * P, P)]).then_inc(ld_mixed[b], 16)
                sp.dma_start(xin[:, b], x_rows[bass.ds(t * P, P), :]).then_inc(ld_xin[b], 16)

            def store(t, b):
                sp.wait_ge(x2_ready, t + 1)
                sp.dma_start(x2_dram[bass.ds(t * P, P), :], x2[:, b]).then_inc(st_x2[b], 16)
                sp.wait_ge(xs_ready, t + 1)
                sp.dma_start(xs_dram[bass.ds(t * P, P), :], xs[:, b]).then_inc(st_xs[b], 16)

            load(0, 0)
            load(1, 1)
            with sp.Fori(0, (NT - 2) // 2) as i:
                for b in range(2):
                    sp.wait_ge(attn_added, i * 2 + (b + 1))
                    sp.wait_ge(conv_done, i * 2 + (b + 1))
                    load(i * 2 + (2 + b), b)
                    store(i * 2 + b, b)
            store(NT - 2, 0)
            store(NT - 1, 1)
            for b in range(2):
                sp.wait_ge(st_x2[b], 16 * NT // 2)
                sp.wait_ge(st_xs[b], 16 * NT // 2)

        @block.tensor
        def _(pe):
            ident = cst[:, C_ID:C_ID + P]

            def part(h, b, done):
                for k in range(h * NCH, (h + 1) * NCH):
                    for j, (m, w) in enumerate(((mhi, whi), (mlo, whi), (mhi, wlo))):
                        for n in range(2):
                            ins = pe.matmul(product[h][:, n], m[:, b, k], w[:, k, n * 512:(n + 1) * 512],
                                            start=k == h * NCH and j == 0, stop=k == (h + 1) * NCH - 1 and j == 2)
                ins.then_inc(done, 1)

            def sum_squares(t, b):
                pe.wait_ge(m_reduced, t + 1)
                pe.wait_ge(m_mean, t)
                for h in range(2):
                    ins = pe.matmul(sums[:, h:h + 1], sqs[:, h], cst[:, C_ONE:C_ONE + 1], start=True, stop=True)
                ins.then_inc(m_summed, 1)

            def turn_x(t, b):
                pe.wait_ge(xs_ready, t + 1)
                pe.wait_ge(x_copied, t)
                for k in range(KD):
                    ins = pe.transpose(turn[:, k // 4, (k % 4) * P:(k % 4 + 1) * P], xs[:, b, k * P:(k + 1) * P],
                                       ident)
                ins.then_inc(x_turned, 1)

            def route(t, b):
                pe.wait_ge(x_copied, t + 1)
                pe.wait_ge(logit_ready, t)
                for k in range(KD):
                    ins = pe.matmul(logit_bank, xT[:, b, k], wrs[:, k], start=k == 0, stop=k == KD - 1)
                ins.then_inc(routed, 1)

            def step(t, b):
                pe.wait_ge(mhi_ready, t + 1)
                pe.wait_ge(mlo_ready, t + 1)
                pe.wait_ge(attn_added, t)
                part(0, b, attn_done)
                if not isinstance(t, int) or t < NT - 1:
                    sum_squares(t + 1, 1 - b)
                if not isinstance(t, int) or t >= 2:
                    route(t - 2, b)
                pe.wait_ge(x2_ready, t)
                part(1, b, conv_done)
                if not isinstance(t, int) or t >= 1:
                    turn_x(t - 1, 1 - b)

            pe.wait_ge(shift_ready, 1)
            for k in range(KD):
                ins = pe.matmul(logit_bank, shift[:, k], wr[:, k], start=k == 0, stop=k == KD - 1)
            ins.then_inc(rbias_done, 1)
            sum_squares(0, 0)
            pe.wait_ge(whi_ready, 2 * NCH)
            pe.wait_ge(wlo_ready, 2 * NCH)
            tiles(pe, step)
            route(NT - 2, 0)
            turn_x(NT - 1, 1)
            route(NT - 1, 1)

        @block.vector
        def _(ve):
            def reduce_squares(t, b):
                ve.wait_ge(m_squared, t + 1)
                ve.wait_ge(m_summed, t)
                ve.tensor_reduce(sqs[:].unsqueeze(3), sq[:].rearrange("p (h k) n -> p h n k", h=2), AX.X, ALU.add
                                 ).then_inc(m_reduced, 1)

            def mixers_scale(t, b):
                ve.wait_ge(m_summed, t + 1)
                ve.tensor_scalar(mstat[:, b, 0], sums, 1 / ATTN, EPS, ALU.mult, ALU.add).then_inc(m_mean, 1)
                ve.wait_ge(m_mean, t + 1)
                ve.reciprocal(mstat[:, b, 0], mstat[:, b, 0]).then_inc(m_inverse, 1)

            def add_attention(t, b):
                ve.wait_ge(attn_done, t + 1)
                ve.wait_ge(m_scale, t + 1)
                ve.wait_ge(ld_xin[b], uses(t, b) + 16)
                ve.wait_ge(st_x2[b], uses(t, b))
                ve.scalar_tensor_tensor(x2[:, b], product[0].rearrange("p a n -> p (a n)"), mstat[:, b, 1, 0:1],
                                        xin[:, b], ALU.mult, ALU.add).then_inc(attn_added, 1)

            def add_conv(t, b):
                ve.wait_ge(conv_done, t + 1)
                ve.wait_ge(attn_added, t + 1)
                ve.scalar_tensor_tensor(x2[:, b], product[1].rearrange("p a n -> p (a n)"), mstat[:, b, 1, 1:2],
                                        x2[:, b], ALU.mult, ALU.add).then_inc(x2_ready, 1)
                ve.wait_ge(x2_squared, t + 1)
                ve.tensor_scalar(xstat[:, b, 1:2], xstat[:, b, 0:1], 1 / D, EPS, ALU.mult, ALU.add
                                 ).then_inc(mean_x, 1)
                ve.wait_ge(mean_x, t + 1)
                ve.reciprocal(xstat[:, b, 1:2], xstat[:, b, 1:2]).then_inc(x2_inverse, 1)
                ve.wait_ge(x2_scale, t + 1)
                ve.wait_ge(st_xs[b], uses(t, b))
                ve.tensor_scalar(xs[:, b], x2[:, b], xstat[:, b, 2:3], None, ALU.mult).then_inc(xs_ready, 1)

            def logit(t, b):
                ve.wait_ge(routed, t + 1)
                out = logits[:, t] if isinstance(t, int) else logits[:, bass.ds(t, 1)].rearrange("p a n -> p (a n)")
                ve.tensor_tensor(out, logit_bank, rbias[:], ALU.add).then_inc(logit_ready, 1)

            def step(t, b):
                last = isinstance(t, int) and t == NT - 1
                if not last:
                    reduce_squares(t + 1, 1 - b)
                add_attention(t, b)
                if not last:
                    mixers_scale(t + 1, 1 - b)
                if not isinstance(t, int) or t >= 2:
                    logit(t - 2, b)
                add_conv(t, b)

            ve.wait_ge(ld_r, 16 * 4)
            for k in range(KD):
                ve.tensor_scalar(wrs[:, k], wr[:, k], modc[:, 24 + k:25 + k], None, ALU.mult)
                ins = ve.tensor_scalar(shift[:, k], cst[:, C_ONE:C_ONE + P], modc[:, 16 + k:17 + k], None, ALU.mult)
            ins.then_inc(shift_ready, 1)
            ve.wait_ge(ld_wout, 16)
            for k in range(2 * NCH):
                gain = cols[:, R_AO + k:R_AO + k + 1]
                ve.scalar_tensor_tensor(wout[:, k], wout[:, k], gain, g1row[:], ALU.mult, ALU.mult
                                        ).then_inc(folded, 1)
                if k:
                    ve.wait_ge(whi_ready, k)
                    ve.tensor_tensor(wlo[:, k - 1], wout[:, k - 1], whi[:, k - 1].bitcast(F32), ALU.subtract
                                     ).then_inc(wlo_ready, 1)
            ve.wait_ge(whi_ready, 2 * NCH)
            ve.tensor_tensor(wlo[:, 2 * NCH - 1], wout[:, 2 * NCH - 1], whi[:, 2 * NCH - 1].bitcast(F32),
                             ALU.subtract).then_inc(wlo_ready, 1)
            ve.wait_ge(rbias_done, 1)
            ve.tensor_tensor(rbias[:], logit_bank, rbias[:], ALU.add)
            reduce_squares(0, 0)
            mixers_scale(0, 0)
            tiles(ve, step)
            logit(NT - 2, 0)
            logit(NT - 1, 1)

        @block.scalar
        def _(act):
            def mixers_in(t, b):
                hold(act, ld_mixed[b], uses(t, b) + 16, passed)
                hold(act, conv_done, t - 1 if not isinstance(t, int) or t >= 2 else 0, passed)
                act.activation(mhi[:, b], mixed[:, b], ACT.Copy).then_inc(mhi_ready, 1)
                act.wait_ge(m_reduced, t)
                act.activation(sq[:], mixed[:, b], ACT.Square).then_inc(m_squared, 1)

            def mixers_scale(t, b):
                act.wait_ge(m_inverse, t + 1)
                act.activation(mstat[:, b, 1], mstat[:, b, 0], ACT.Sqrt).then_inc(m_scale, 1)

            def copy_x(t, b):
                act.wait_ge(x_turned, t + 1)
                act.activation(xT[:, b].rearrange("p k n -> p (k n)"), turn.rearrange("p a n -> p (a n)"), ACT.Copy
                               ).then_inc(x_copied, 1)

            def step(t, b):
                last = isinstance(t, int) and t == NT - 1
                if not last:
                    mixers_in(t + 1, 1 - b)
                    mixers_scale(t + 1, 1 - b)
                act.wait_ge(x2_ready, t + 1)
                act.activation(junk[:], x2[:, b], ACT.Square, accum_out=xstat[:, b, 0:1]).then_inc(x2_squared, 1)
                act.wait_ge(x2_inverse, t + 1)
                act.activation(xstat[:, b, 2:3], xstat[:, b, 1:2], ACT.Sqrt).then_inc(x2_scale, 1)
                if not isinstance(t, int) or t >= 1:
                    copy_x(t - 1, 1 - b)

            mixers_in(0, 0)
            for k in range(2 * NCH):
                act.wait_ge(folded, k + 1)
                act.activation(whi[:, k], wout[:, k], ACT.Copy).then_inc(whi_ready, 1)
            mixers_scale(0, 0)
            tiles(act, step)
            copy_x(NT - 1, 1)

        @block.gpsimd
        def _(po):
            def step(t, b):
                hold(po, mhi_ready, t + 1, passed_pool)
                po.tensor_tensor(mlo[:, b], mixed[:, b], mhi[:, b].bitcast(F32), ALU.subtract
                                 ).then_inc(mlo_ready, 1)

            tiles(po, step)


def route(nc, T, st):
    with ExitStack() as ctx:
        sb = lambda name, shape, dt=F32: ctx.enter_context(nc.sbuf_tensor(name, shape, dt))
        sem = lambda name: ctx.enter_context(nc.semaphore(name))
        cst, logits, gates, rank, marks, rounds = (st[k] for k in (
            "cst", "logits", "gates", "rank", "marks", "rounds"))
        g1, gexp, gcand, gone, gpen = (sb(n, [P, NT, NGRP]) for n in ("g1", "gexp", "gcand", "gone", "gpen"))
        best, pgrp, low = sb("best", [P, 2, NT, 1]), sb("pgrp", [P, NT, 1]), sb("low", [P, NT, 1])
        em, cand = sb("em", [P, NT, NEXP]), sb("cand", [P, NT, NEXP])
        pick = sb("pick", [P, NT, 2, NEXP])
        tmp = sb("tmp", [P, NT, 2, NEXP])
        both = sb("both", [P, NT * NEXP], BF16)
        trib, oneb = sb("trib", [P, P], BF16), sb("oneb", [P, P], BF16)
        dexp = sb("dexp", [P, NT, 1])
        most, need, need1 = sb("most", [P, 1]), sb("need", [P, ROUNDS]), sb("need1", [P, 1])
        bank = ctx.enter_context(nc.psum_tensor("rbank", [P, 2, 512], F32))
        dve_step, less_best, group_exp, pair_less, pair_exp = (sem(n) for n in (
            "dve_step4", "less_best", "group_exp", "pair_less", "pair_exp"))
        both_ready, ranked = sem("both_ready"), sem("ranked")
        block = ctx.enter_context(nc.Block())

        def across(ap, n, k):
            return ap.to_broadcast([P, n, k])

        def repeat(ap, n):
            return ap.unsqueeze(1).to_broadcast([P, n, ap.shape[-1]])

        @block.vector
        def _(ve):
            V = Steps(ve, dve_step)

            def do(ins, sem=None):
                V(ins, sem)
                V.wait()

            G, E = logits[:, :, 0:NGRP], logits[:, :, NGRP:]
            top = best[:, 0]
            do(ve.tensor_copy(trib[:], cst[:, C_TRI:C_TRI + P]))
            do(ve.tensor_copy(oneb[:], cst[:, C_ONE:C_ONE + P]))
            do(ve.tensor_reduce(top, G, AX.X, ALU.max))
            do(ve.tensor_tensor(g1[:], G, across(top, NT, NGRP), ALU.subtract), less_best)
            do(ve.tensor_tensor(gone[:], G, across(top, NT, NGRP), ALU.is_equal))
            do(ve.scalar_tensor_tensor(gcand[:], gone[:], -64.0, repeat(cst[:, C_GRP:C_GRP + NGRP], NT),
                                       ALU.mult, ALU.add))
            do(ve.tensor_reduce(low[:], gcand[:], AX.X, ALU.min))
            do(ve.tensor_tensor(gone[:], gcand[:], across(low[:], NT, NGRP), ALU.is_equal))
            do(ve.tensor_scalar(gpen[:], gone[:], BIG, BIG, ALU.mult, ALU.subtract))
            ve.wait_ge(group_exp, 1)
            do(ve.tensor_reduce(pgrp[:], gexp[:], AX.X, ALU.add))
            do(ve.reciprocal(pgrp[:], pgrp[:]))
            in_groups = lambda ap: ap.rearrange("p t (g e) -> p t g e", g=NGRP)
            on_experts = lambda ap: ap.unsqueeze(3).to_broadcast([P, NT, NGRP, EPG])
            do(ve.tensor_tensor(in_groups(em[:]), in_groups(E), on_experts(gone[:]), ALU.mult))
            do(ve.tensor_tensor(in_groups(em[:]), in_groups(em[:]), on_experts(gpen[:]), ALU.add))
            for k in range(2):
                m = best[:, k]
                do(ve.tensor_reduce(m, em[:], AX.X, ALU.max))
                do(ve.tensor_tensor(cand[:], em[:], across(m, NT, NEXP), ALU.is_equal))
                do(ve.scalar_tensor_tensor(cand[:], cand[:], -64.0, repeat(cst[:, C_EXP:C_EXP + NEXP], NT),
                                           ALU.mult, ALU.add))
                do(ve.tensor_reduce(low[:], cand[:], AX.X, ALU.min))
                do(ve.tensor_tensor(pick[:, :, k], cand[:], across(low[:], NT, NEXP), ALU.is_equal))
                if k == 0:
                    do(ve.scalar_tensor_tensor(em[:], pick[:, :, 0], -3 * BIG, em[:], ALU.mult, ALU.add))
            do(ve.tensor_tensor(both[:].rearrange("p (t e) -> p t e", t=NT), pick[:, :, 0], pick[:, :, 1], ALU.add),
               both_ready)
            do(ve.tensor_tensor(dexp[:], best[:, 1], best[:, 0], ALU.subtract), pair_less)
            ve.wait_ge(pair_exp, 1)
            do(ve.tensor_scalar(low[:], dexp[:], 1.0, None, ALU.add))
            do(ve.reciprocal(low[:], low[:]))
            do(ve.tensor_tensor(gates[:, 0::2].unsqueeze(2), low[:], pgrp[:], ALU.mult))
            do(ve.tensor_tensor(gates[:, 1::2].unsqueeze(2), gates[:, 0::2].unsqueeze(2), dexp[:], ALU.mult))
            for k in range(2):
                do(ve.tensor_tensor(marks[:, :, k, 0:NEXP], pick[:, :, k],
                                    cst[:, C_SLOT:C_SLOT + NT].unsqueeze(2).to_broadcast([P, NT, NEXP]), ALU.mult))
                do(ve.tensor_scalar(marks[:, :, k, 2 * NEXP:], pick[:, :, k], float(1 + k), None, ALU.mult))
                do(ve.tensor_scalar(marks[:, :, k, NEXP:2 * NEXP], pick[:, :, k], cst[:, C_PART:C_PART + 1], None, ALU.mult))
            ve.wait_ge(ranked, 1)
            before = bank[:, 0].rearrange("p (t e) -> p t e", t=NT)
            for k in range(2):
                do(ve.tensor_tensor(tmp[:, :, k], pick[:, :, k], before, ALU.mult))
            do(ve.tensor_reduce(rank[:].rearrange("p (t k) -> p t k", k=2), tmp[:], AX.X, ALU.add))
            do(ve.tensor_reduce(most[:], bank[:, 1, 0:NEXP], AX.X, ALU.max))
            do(ve.tensor_scalar(need[:], cst[:, C_RND:C_RND + ROUNDS], most[:], None, ALU.is_lt))
            do(ve.tensor_reduce(need1[:], need[:], AX.X, ALU.add))
            do(ve.tensor_copy(rounds[:], need1[:]))

        @block.scalar
        def _(act):
            act.wait_ge(less_best, 1)
            act.activation(gexp[:], g1[:], ACT.Exp).then_inc(group_exp, 1)
            act.wait_ge(pair_less, 1)
            act.activation(dexp[:], dexp[:], ACT.Exp).then_inc(pair_exp, 1)

        @block.tensor
        def _(pe):
            pe.wait_ge(both_ready, 1)
            pe.matmul(bank[:, 0], trib[:], both[:], start=True, stop=False)
            for j in range(1, NT):
                pe.matmul(bank[:, 0, j * NEXP:], oneb[:], both[:, 0:(NT - j) * NEXP], start=False, stop=j == NT - 1)
            for t in range(NT):
                ins = pe.matmul(bank[:, 1, 0:NEXP], oneb[:], both[:, t * NEXP:(t + 1) * NEXP],
                                start=t == 0, stop=t == NT - 1)
            ins.then_inc(ranked, 1)


def experts(nc, T, st):
    with ExitStack() as ctx:
        sb = lambda name, shape, dt=F32: ctx.enter_context(nc.sbuf_tensor(name, shape, dt))
        sem = lambda name: ctx.enter_context(nc.semaphore(name))
        cst, modc, rank, marks, rounds, xs_dram, y_dram = (st[k] for k in (
            "cst", "modc", "rank", "marks", "rounds", "xs_dram", "y_dram"))
        inslot = sb("inslot", [P, NT * 2, CAP], BF16)
        slot_a, slot_b = sb("slot_a", [P, NEXP + 1], I32), sb("slot_b", [CAPB, NEXP + 1], I32)
        dest_a, dest_b = sb("dest_a", [P, NEXP], I32), sb("dest_b", [CAPB, NEXP], I32)
        tab_a, tab_b = sb("tab_a", [P, 3 * NEXP]), sb("tab_b", [CAPB, 3 * NEXP])
        dump_b, row_a, row_b = sb("dump_b", [CAPB, NEXP]), sb("row_a", [P, NEXP]), sb("row_b", [CAPB, NEXP])
        ia, ib = sb("ia", [P, 2], I32), sb("ib", [CAPB, 2], I32)
        ja, jb = sb("ja", [P, 2], I32), sb("jb", [CAPB, 2], I32)
        xa, xb = sb("xa", [P, 2, D]), sb("xb", [CAPB, 2, D])
        xT = sb("xTe", [P, 2, KD, CAP])
        wg, wu, wd = sb("wg", [P, 2, KD, FE]), sb("wu", [P, 2, KD, FE]), sb("wd", [P, 2, KF, D])
        sg, aT = sb("sg", [P, KF, CAP]), sb("aT", [P, KF, CAP])
        ya, yb = sb("ya", [P, 2, D]), sb("yb", [CAPB, 2, D])
        bank = ctx.enter_context(nc.psum_tensor("ebank", [P, 8, 512], F32))
        turn, gate, up, outa, outb = bank[:, 0:2], bank[:, 2], bank[:, 3], bank[:, 4:6], bank[0:CAPB, 6:8]

        slots_ready, table_summed, table_ready = sem("slots_ready"), sem("table_summed"), sem("table_ready")
        idx_copied, dest_copied = sem("idx_copied"), sem("dest_copied")
        gathered, turned = [sem("gathered0"), sem("gathered1")], [sem("xturned0"), sem("xturned1")]
        ld_exp = [sem("ld_exp0"), sem("ld_exp1")]
        turn_dve, turn_act = sem("turn_dve"), sem("turn_act")
        gate_done, up_done, silu_done, act_done = sem("gate_done"), sem("up_done"), sem("silu_done5"), sem("mlp_done")
        down_a, down_b, ya_done, yb_done = sem("down_a"), sem("down_b"), sem("ya_done"), sem("yb_done")
        st_ya, st_yb = [sem("st_ya0"), sem("st_ya1")], [sem("st_yb0"), sem("st_yb1")]
        dve_step, dump_ready = sem("dve_step5"), sem("dump_ready")
        passed, passed_pool = sem("passed5"), sem("passed_pool5")
        block = ctx.enter_context(nc.Block())
        PAIRS = NEXP // 2
        TURNS = NEXP + 1

        def load_rounds(eng):
            return eng.value_load(rounds[0:1, 0:1], min_val=1, max_val=ROUNDS)

        @block.sync
        def _(sp):
            n_rounds = load_rounds(sp)
            wgd = T["w_exp_gate"].rearrange("l e (k p) n -> p (l e k) n", p=P)
            wud = T["w_exp_up"].rearrange("l e (k p) n -> p (l e k) n", p=P)
            wdd = T["w_exp_down"].rearrange("l e (k p) n -> p (l e k) n", p=P)
            with sp.Fori(0, n_rounds) as r:
                with sp.Fori(0, PAIRS) as ep:
                    for b in range(2):
                        sp.wait_ge(down_b, r * NEXP + ep * 2 + (b + 1))
                        sp.dma_start(wg[:, b], wgd[:, bass.ds(ep * 2 * KD + b * KD, KD), :]).then_inc(ld_exp[b], 16)
                        sp.dma_start(wu[:, b], wud[:, bass.ds(ep * 2 * KD + b * KD, KD), :]).then_inc(ld_exp[b], 16)
                        sp.dma_start(wd[:, b], wdd[:, bass.ds(ep * 2 * KF + b * KF, KF), :]).then_inc(ld_exp[b], 16)

        @block.gpsimd
        def _(po):
            n_rounds = load_rounds(po)

            def gather(b, column, use, copied):
                hold(po, turned[b], use * 4, passed_pool)
                po.tensor_copy(ia[:, b:b + 1], slot_a[:, bass.ds(column, 1)]).then_inc(idx_copied, 1)
                po.tensor_copy(ib[:, b:b + 1], slot_b[:, bass.ds(column, 1)]).then_inc(idx_copied, 1)
                hold(po, idx_copied, copied * 2 + 2, passed_pool)
                for x, i in ((xa, ia), (xb, ib)):
                    po.indirect_dma_start(out=x[:, b], out_offset=None, in_=xs_dram,
                                          in_offset=bass.IndirectOffsetOnAxis(ap=i[:, b:b + 1], axis=0)
                                          ).then_inc(gathered[b], 16)

            def scatter(b, column, use, e):
                hold(po, st_ya[b], use * 16, passed_pool)
                hold(po, st_yb[b], use * 16, passed_pool)
                po.tensor_copy(ja[:, b:b + 1], dest_a[:, bass.ds(column, 1)]).then_inc(dest_copied, 1)
                po.tensor_copy(jb[:, b:b + 1], dest_b[:, bass.ds(column, 1)]).then_inc(dest_copied, 1)
                hold(po, dest_copied, e * 2 + 2, passed_pool)
                for y, j, done, stored in ((ya, ja, ya_done, st_ya), (yb, jb, yb_done, st_yb)):
                    hold(po, done, e + 1, passed_pool)
                    po.indirect_dma_start(out=y_dram, in_=y[:, b], in_offset=None,
                                          out_offset=bass.IndirectOffsetOnAxis(ap=j[:, b:b + 1], axis=0)
                                          ).then_inc(stored[b], 16)

            with po.Fori(0, n_rounds) as r:
                hold(po, table_ready, r * 6 + 6, passed_pool)
                gather(0, r * 0, r * (PAIRS + 1), r * TURNS)
                gather(1, r * 0 + 1, r * PAIRS, r * TURNS + 1)
                with po.Fori(0, PAIRS - 1) as ep:
                    for b in range(2):
                        gather(b, ep * 2 + (2 + b), r * (PAIRS + 1 - b) + ep + 1, r * TURNS + ep * 2 + (2 + b))
                        scatter(b, ep * 2 + b, r * PAIRS + ep, r * NEXP + ep * 2 + b)
                gather(0, r * 0 + NEXP, r * (PAIRS + 1) + PAIRS, r * TURNS + NEXP)
                for b in range(2):
                    scatter(b, r * 0 + (NEXP - 2 + b), r * PAIRS + (PAIRS - 1), r * NEXP + (NEXP - 2 + b))
            for b in range(2):
                hold(po, st_ya[b], n_rounds * (PAIRS * 16), passed_pool)
                hold(po, st_yb[b], n_rounds * (PAIRS * 16), passed_pool)

        @block.tensor
        def _(pe):
            n_rounds = load_rounds(pe)
            ident = cst[:, C_ID:C_ID + P]

            def turn_in(b, groups, use, seq):
                for g in groups:
                    if g == 0:
                        pe.wait_ge(gathered[b], use * 32 + 32)
                    pe.wait_ge(turn_act if g % 2 else turn_dve, seq * 4 + g // 2 * 2)
                    for j in range(2):
                        k = 2 * g + j
                        pe.transpose(turn[:, g % 2, j * CAP:j * CAP + P], xa[:, b, k * P:(k + 1) * P], ident)
                        ins = pe.transpose(turn[:, g % 2, j * CAP + P:(j + 1) * CAP], xb[:, b, k * P:(k + 1) * P],
                                           cst[0:CAPB, C_ID:C_ID + CAPB])
                    ins.then_inc(turned[b], 1)

            pe.sem_inc(down_b, 2)
            with pe.Fori(0, n_rounds) as r:
                pe.wait_ge(slots_ready, r + 1)
                pe.wait_ge(ya_done, r * NEXP)
                for out, lo, n in ((bank[:, 4, 0:3 * NEXP], 0, P), (bank[0:CAPB, 5, 0:3 * NEXP], P, CAPB)):
                    for j in range(NT * 2):
                        ins = pe.matmul(out, inslot[:, j, lo:lo + n],
                                        marks[:, j // 2, j % 2], start=j == 0, stop=j == NT * 2 - 1)
                    ins.then_inc(table_summed, 1)
                turn_in(0, range(4), r * (PAIRS + 1), r * TURNS)
                with pe.Fori(0, PAIRS) as ep:
                    for b in range(2):
                        e = r * NEXP + ep * 2 + b
                        seq = r * TURNS + ep * 2 + b
                        pe.wait_ge(ld_exp[b], r * (PAIRS * 48) + ep * 48 + 48)
                        pe.wait_ge(turn_dve, seq * 4 + 4)
                        pe.wait_ge(turn_act, seq * 4 + 4)
                        for w, out, done in ((wg, gate, gate_done), (wu, up, up_done)):
                            for f in range(KF):
                                for k in range(KD):
                                    ins = pe.matmul(out[:, f * CAP:(f + 1) * CAP], w[:, b, k, f * P:(f + 1) * P],
                                                    xT[:, b, k], start=k == 0, stop=k == KD - 1)
                            ins.then_inc(done, 1)
                        nxt = (1 - b, r * (PAIRS + b) + ep + b, seq + 1)
                        turn_in(nxt[0], (0, 1), nxt[1], nxt[2])
                        pe.wait_ge(act_done, e + 1)
                        pe.wait_ge(ya_done, e)
                        for n in range(2):
                            for f in range(KF):
                                ins = pe.matmul(outa[:, n], aT[:, f, 0:P], wd[:, b, f, n * 512:(n + 1) * 512],
                                                start=f == 0, stop=f == KF - 1)
                        ins.then_inc(down_a, 1)
                        turn_in(nxt[0], (2, 3), nxt[1], nxt[2])
                        pe.wait_ge(yb_done, e)
                        for n in range(2):
                            for f in range(KF):
                                ins = pe.matmul(outb[:, n], aT[:, f, P:CAP], wd[:, b, f, n * 512:(n + 1) * 512],
                                                start=f == 0, stop=f == KF - 1)
                        ins.then_inc(down_b, 1)

        @block.vector
        def _(ve):
            n_rounds = load_rounds(ve)

            def copy_in(b, groups, use):
                for g in groups:
                    ve.wait_ge(turned[b], use * 4 + g + 1)
                    for j in range(2):
                        k = 2 * g + j
                        ve.tensor_scalar(xT[:, b, k], turn[:, 0, j * CAP:(j + 1) * CAP], modc[:, 24 + k:25 + k],
                                         modc[:, 16 + k:17 + k], ALU.mult, ALU.add).then_inc(turn_dve, 1)

            ve.tensor_scalar(dump_b[:], cst[0:CAPB, C_DUMP:C_DUMP + NEXP], float(P), None, ALU.add
                             ).then_inc(dump_ready, 1)
            with ve.Fori(0, n_rounds) as r:
                ve.wait_ge(table_summed, r * 2)
                ve.wait_ge(dve_step, r * 9)
                ve.tensor_tensor(inslot[:], cst[:, C_SLOT:C_SLOT + CAP].unsqueeze(1).to_broadcast([P, NT * 2, CAP]),
                                 rank[:].unsqueeze(2).to_broadcast([P, NT * 2, CAP]), ALU.is_equal
                                 ).then_inc(slots_ready, 1)
                ve.wait_ge(slots_ready, r + 1)
                ve.tensor_scalar(rank[:], rank[:], float(-CAP), None, ALU.add).then_inc(dve_step, 1)
                ve.wait_ge(idx_copied, r * (TURNS * 2))
                ve.wait_ge(dest_copied, r * (NEXP * 2))
                ve.wait_ge(dump_ready, 1)
                for j, (psum, tab, dump, row, slot, dest) in enumerate((
                        (bank[:, 4], tab_a, cst[:, C_DUMP:C_DUMP + NEXP], row_a, slot_a, dest_a),
                        (bank[0:CAPB, 5], tab_b, dump_b[:], row_b, slot_b, dest_b))):
                    tile, in_tile, mark = (tab[:, n * NEXP:(n + 1) * NEXP] for n in range(3))
                    ve.wait_ge(table_summed, r * 2 + (j + 1))
                    ve.wait_ge(dve_step, r * 9 + (4 * j + 1))
                    ve.tensor_copy(tab[:], psum[:, 0:3 * NEXP]).then_inc(dve_step, 1)
                    ve.wait_ge(dve_step, r * 9 + (4 * j + 2))
                    ve.scalar_tensor_tensor(slot[:, 0:NEXP], tile, float(P), in_tile, ALU.mult, ALU.add
                                            ).then_inc(table_ready, 1)
                    ve.scalar_tensor_tensor(row[:], mark, 0.0, dump, ALU.is_equal, ALU.mult).then_inc(dve_step, 1)
                    ve.wait_ge(dve_step, r * 9 + (4 * j + 3))
                    ve.tensor_tensor(row[:], row[:], mark, ALU.add).then_inc(dve_step, 1)
                    ve.wait_ge(dve_step, r * 9 + (4 * j + 4))
                    ve.scalar_tensor_tensor(row[:], in_tile, 2.0, row[:], ALU.mult, ALU.add).then_inc(dve_step, 1)
                    ve.wait_ge(dve_step, r * 9 + (4 * j + 5))
                    ve.scalar_tensor_tensor(dest[:], tile, 2.0 * P, row[:], ALU.mult, ALU.add
                                            ).then_inc(table_ready, 1)
                ve.wait_ge(table_ready, r * 6 + 4)
                ve.tensor_copy(slot_a[:, NEXP:], slot_a[:, 0:1]).then_inc(table_ready, 1)
                ve.tensor_copy(slot_b[:, NEXP:], slot_b[:, 0:1]).then_inc(table_ready, 1)
                copy_in(0, (0, 2), r * (PAIRS + 1))
                with ve.Fori(0, PAIRS) as ep:
                    for b in range(2):
                        e = r * NEXP + ep * 2 + b
                        ve.wait_ge(up_done, e + 1)
                        ve.wait_ge(silu_done, e + 1)
                        ve.tensor_tensor(aT[:].rearrange("p f n -> p (f n)"), sg[:].rearrange("p f n -> p (f n)"),
                                         up[:, 0:KF * CAP], ALU.mult).then_inc(act_done, 1)
                        copy_in(1 - b, (0, 2), r * (PAIRS + b) + ep + b)
                        ve.wait_ge(down_b, e + 3)
                        ve.wait_ge(st_yb[b], r * (PAIRS * 16) + ep * 16)
                        ve.tensor_copy(yb[:, b], outb.rearrange("p a n -> p (a n)")).then_inc(yb_done, 1)

        @block.scalar
        def _(act):
            n_rounds = load_rounds(act)

            def copy_in(b, groups, use):
                for g in groups:
                    act.wait_ge(turned[b], use * 4 + g + 1)
                    for j in range(2):
                        k = 2 * g + j
                        act.activation(xT[:, b, k], turn[:, 1, j * CAP:(j + 1) * CAP], ACT.Identity,
                                       scale=modc[:, 24 + k:25 + k], bias=modc[:, 16 + k:17 + k]
                                       ).then_inc(turn_act, 1)

            with act.Fori(0, n_rounds) as r:
                copy_in(0, (1, 3), r * (PAIRS + 1))
                with act.Fori(0, PAIRS) as ep:
                    for b in range(2):
                        e = r * NEXP + ep * 2 + b
                        use = r * (PAIRS + b) + ep + b
                        act.wait_ge(gate_done, e + 1)
                        act.activation(sg[:].rearrange("p f n -> p (f n)"), gate[:, 0:KF * CAP], ACT.Silu
                                       ).then_inc(silu_done, 1)
                        copy_in(1 - b, (1,), use)
                        act.wait_ge(down_a, e + 1)
                        act.wait_ge(st_ya[b], r * (PAIRS * 16) + ep * 16)
                        act.activation(ya[:, b], outa.rearrange("p a n -> p (a n)"), ACT.Copy).then_inc(ya_done, 1)
                        copy_in(1 - b, (3,), use)


def combine(nc, T, st, out):
    with ExitStack() as ctx:
        sb = lambda name, shape, dt=F32: ctx.enter_context(nc.sbuf_tensor(name, shape, dt))
        sem = lambda name: ctx.enter_context(nc.semaphore(name))
        g2row, fgrow, gates, x2_dram, y_dram = (st[k] for k in ("g2row", "fgrow", "gates", "x2_dram", "y_dram"))
        y, x2, res = sb("y", [P, 2, 2, D]), sb("x2f", [P, 2, D]), sb("res", [P, 2, D])
        junk = sb("junkf", [P, D])
        stat = sb("statf", [P, 2, 3])
        ld_y, ld_x2, st_out = ([sem(f"{n}{b}") for b in range(2)] for n in ("ld_y", "ld_x2", "st_out"))
        first_gated, summed, gated, added = (sem(n) for n in (
            "first_gated", "y_summed", "y_gated", "added"))
        squared, mean, inverse, scale, normed = (sem(n) for n in (
            "squared6", "mean6", "inverse6", "scale6", "normed"))
        passed = sem("passed6")
        block = ctx.enter_context(nc.Block())
        out_rows = out.rearrange("b s d -> (b s) d")

        pairs = y_dram[1:1 + 2 * S, :].rearrange("(t k) d -> t k d", k=2)

        @block.sync
        def _(sp):
            def load(t, b):
                sp.dma_start(y[:, b], pairs[bass.ds(t * P, P)]).then_inc(ld_y[b], 16)
                sp.dma_start(x2[:, b], x2_dram[bass.ds(t * P, P), :]).then_inc(ld_x2[b], 16)

            for b in range(2):
                load(b, b)
            with sp.Fori(0, NT // 2 - 1) as i:
                for b in range(2):
                    sp.wait_ge(normed, i * 2 + (b + 1))
                    sp.dma_start(out_rows[bass.ds(i * 2 * P + b * P, P), :], res[:, b]).then_inc(st_out[b], 16)
                    load(i * 2 + (b + 2), b)
            for b in range(2):
                t = NT - 2 + b
                sp.wait_ge(normed, t + 1)
                sp.dma_start(out_rows[t * P:(t + 1) * P, :], res[:, b]).then_inc(st_out[b], 16)
            for b in range(2):
                sp.wait_ge(st_out[b], 16 * NT // 2)

        @block.scalar
        def _(act):
            with act.Fori(0, NT // 2) as i:
                for b in range(2):
                    hold(act, ld_y[b], i * 16 + 16, passed)
                    act.activation(y[:, b, 0], y[:, b, 0], ACT.Copy, scale=gates[:, bass.ds(i * 4 + 2 * b, 1)]
                                   ).then_inc(first_gated, 1)
                    act.wait_ge(added, i * 2 + (b + 1))
                    act.activation(junk[:], x2[:, b], ACT.Square, accum_out=stat[:, b, 0:1]).then_inc(squared, 1)
                    act.wait_ge(inverse, i * 2 + (b + 1))
                    act.activation(stat[:, b, 2:3], stat[:, b, 1:2], ACT.Sqrt).then_inc(scale, 1)

        @block.vector
        def _(ve):
            with ve.Fori(0, NT // 2) as i:
                for b in range(2):
                    n = i * 2 + (b + 1)
                    ve.wait_ge(first_gated, n)
                    ve.wait_ge(ld_y[b], i * 16 + 16)
                    ve.scalar_tensor_tensor(y[:, b, 1], y[:, b, 1], gates[:, bass.ds(i * 4 + (2 * b + 1), 1)], y[:, b, 0],
                                            ALU.mult, ALU.add).then_inc(summed, 1)
                    ve.wait_ge(summed, n)
                    ve.tensor_tensor(y[:, b, 0], y[:, b, 1], g2row[:], ALU.mult).then_inc(gated, 1)
                    ve.wait_ge(gated, n)
                    ve.wait_ge(ld_x2[b], i * 16 + 16)
                    ve.tensor_tensor(x2[:, b], x2[:, b], y[:, b, 0], ALU.add).then_inc(added, 1)
                    ve.wait_ge(squared, n)
                    ve.tensor_scalar(stat[:, b, 1:2], stat[:, b, 0:1], 1 / D, EPS, ALU.mult, ALU.add
                                     ).then_inc(mean, 1)
                    ve.wait_ge(mean, n)
                    ve.reciprocal(stat[:, b, 1:2], stat[:, b, 1:2]).then_inc(inverse, 1)
                    ve.wait_ge(scale, n)
                    ve.wait_ge(st_out[b], i * 16)
                    ve.scalar_tensor_tensor(res[:, b], x2[:, b], stat[:, b, 2:3], fgrow[:], ALU.mult, ALU.mult
                                            ).then_inc(normed, 1)


def program(nc, T, out):
    with ExitStack() as whole:
        def tensor(scope, side=None):
            return lambda name, shape, dt=F32: scope.enter_context(nc.sbuf_tensor(name, shape, dt, side=side))

        keep = tensor(whole)
        scratch = lambda name, shape: nc.dram_tensor(name, shape, F32, kind="Internal").ap()
        st = {"cst": keep("cst", [P, C_ALL]), "cols": keep("cols", [P, 96]), "modc": keep("modcol", [P, 32]),
              "g1row": keep("g1row", [P, D]), "g2row": keep("g2row", [P, D]), "fgrow": keep("fgrow", [P, D]),
              "mix_dram": scratch("mix_dram", [P, 2 * NCH, S]), "x2_dram": scratch("x2_dram", [S, D]),
              "xs_dram": scratch("xs_dram", [S, D]), "y_dram": scratch("y_dram", [1 + 2 * S + 2 * CAP, D])}
        with ExitStack() as mixers:
            left = tensor(mixers)
            st["cs"] = left("cs", [P, S])
            with ExitStack() as first:
                st["hT"] = tensor(first, "right")("hT", [P, KD, S])
                prepare(nc, T, st)
                st["qn"], st["kvn"], st["KR"] = left("qn", [P, KQ, S]), left("kvn", [P, S]), left("KR", [P, S])
                project(nc, T, st)
            attend(nc, T, st)
        st["logits"] = keep("logits", [P, NT, NGRP + NEXP])
        mix(nc, T, st)
        st["gates"], st["rank"] = keep("gates", [P, NT * 2]), keep("rank", [P, NT * 2])
        st["marks"], st["rounds"] = keep("marks", [P, NT, 2, 3 * NEXP], BF16), keep("rounds", [P, 1], I32)
        route(nc, T, st)
        experts(nc, T, st)
        combine(nc, T, st, out)


_INS = ["x", "c", "positions", "w_ada", "b_ada", "norm1_g", "w_in", "q_norm_g", "kv_norm_g", "w_uq", "w_uk", "w_uv",
        "conv_w", "conv_b", "attn_out_g", "conv_out_g", "w_out", "norm2_g", "w_router_group", "b_router_group",
        "w_router_expert", "b_router_expert", "w_exp_gate", "w_exp_up", "w_exp_down", "final_g"]


def kernel(**inputs):
    import concourse.bacc as bacc
    from concourse.bass_utils import run_bass_kernel_spmd

    nc = bacc.Bacc("TRN2", target_bir_lowering=False, num_devices=1)
    arrays = {f"in_{n}": np.ascontiguousarray(inputs[n]) for n in _INS}
    arrays["in_consts"] = constants()
    T = {n[3:]: nc.dram_tensor(n, a.shape, mybir.dt.from_np(a.dtype), kind="ExternalInput").ap()
         for n, a in arrays.items()}
    out = nc.dram_tensor("out", [1, S, D], F32, kind="ExternalOutput").ap()
    program(nc, T, out)
    r = run_bass_kernel_spmd(nc, [arrays], core_ids=[0])
    return r.results[0]["out"]
```

```python
import math
from contextlib import ExitStack

import numpy as np

import concourse.bass as bass
from concourse import mybir

P = 128
F32 = mybir.dt.float32
F32R = mybir.dt.float32r
BF16 = mybir.dt.bfloat16
I32 = mybir.dt.int32
ALU = mybir.AluOpType
ACT = mybir.ActivationFunctionType
AX = mybir.AxisListType

D = 1024
KD = D // P
S = 2048
NT = S // P
NG = 4
GT = NT // NG
GW = GT * P
HEADS = 8
NOPE = 64
ROPE = 32
QKD = NOPE + ROPE
VD = 64
QR = 256
KQ = QR // P
KVR = 128
ATTN = HEADS * VD
CONV = 512
NCH = CONV // P
TAPS = 3
NEXP = 32
NGRP = 4
EPG = NEXP // NGRP
FE = 256
KF = FE // P
CAP = 192
CAPB = CAP - P
ROUNDS = -(-S // CAP)
EPS = 1e-6
BIG = 1e30
SM = 1.0 / math.sqrt(QKD)

C_ID, C_ONE, C_TRI, C_FOLD = 0, 128, 256, 384
C_FREQ, C_TURN, C_PHASE, C_SIGN, C_PART = 448, 449, 450, 451, 452
C_SLOT, C_EXP, C_GRP, C_RND = 456, 648, 680, 684
C_DUMP = 696
C_ROWS = C_DUMP + NEXP
C_SMALL = C_ROWS
C_ALL = C_ROWS + 1024

R_BADA, R_N1, R_N2, R_AO, R_CO, R_Q, R_KV, R_CW, R_CB, R_ALL = 0, 48, 56, 64, 68, 72, 74, 75, 87, 91

TWO_PI = 2 * math.pi
PI_1 = 6.28125
PI_2 = math.floor((TWO_PI - PI_1) * 2**19) / 2**19
PI_3 = math.floor((TWO_PI - PI_1 - PI_2) * 2**30) / 2**30
PI_4 = TWO_PI - PI_1 - PI_2 - PI_3
ROUND = 1.5 * 2**23
PI_IN = 3.1415925


def constants():
    c = np.zeros((P, C_ALL), np.float32)
    c[:, C_ID:C_ID + P] = np.eye(P)
    c[:, C_ONE:C_ONE + P] = 1
    c[:, C_TRI:C_TRI + P] = np.triu(np.ones((P, P)), 1)
    i = np.arange(64)
    c[64:, C_FOLD:C_FOLD + 64] = (i[:, None] % ROPE) == (i[None] % ROPE)
    freq = np.float32(1) / (np.float64(10000.0) ** (np.arange(0, ROPE, 2) / ROPE)).astype(np.float32)
    c[64:, C_FREQ] = np.tile(freq, 4)
    c[64:96, C_TURN] = 0.25
    c[64:96, C_PHASE] = math.pi / 2
    c[:, C_SIGN] = 1
    c[96:112, C_SIGN] = -1
    c[:, C_PART] = np.arange(P)
    c[:, C_SLOT:C_SLOT + CAP] = np.arange(CAP)
    c[:, C_EXP:C_EXP + NEXP] = np.arange(NEXP)
    c[:, C_GRP:C_GRP + NGRP] = np.arange(NGRP)
    c[:, C_RND:C_RND + ROUNDS] = np.arange(ROUNDS) * CAP
    c[:, C_DUMP:C_DUMP + NEXP] = 1 + 2 * S + np.arange(P)[:, None] + np.arange(NEXP) % 2 * CAP
    c[96, C_ROWS:C_ROWS + 512] = 1
    for j in range(4):
        c[97 + j, C_ROWS + j * P + 64:C_ROWS + (j + 1) * P] = 1
        c[97 + j, C_ROWS + 512 + j * P:C_ROWS + 512 + j * P + 64] = -2.0**100
    return c


class Steps:

    def __init__(self, eng, sem):
        self.eng, self.sem, self.count, self.last = eng, sem, {}, None
        self.it, self.per, self.base = None, {}, {}

    def __call__(self, ins, sem=None):
        sem = sem or self.sem
        ins.then_inc(sem, 1)
        self.count[sem.name] = self.count.get(sem.name, 0) + 1
        self.last = sem

    def wait(self):
        if self.last is not None:
            n = self.count[self.last.name]
            self.eng.wait_ge(self.last, n if self.it is None else self.it * self.per[self.last.name] + n)

    def enter(self, it, per):
        self.it, self.per, self.base, self.last = it, {s.name: n for s, n in per.items()}, dict(self.count), None

    def leave(self, trips):
        self.wait()
        for k, n in self.count.items():
            made = n - self.base.get(k, 0)
            assert made == self.per.get(k, 0), (k, made)
            self.count[k] = n + made * (trips - 1)
        self.it, self.last = None, None


def hold(eng, sem, value, passed):
    eng.wait_ge(sem, value)
    eng.sem_inc(passed, 1)


def rows(v):
    return v.rearrange("l (r c) -> (l r) c", c=P)


def prepare(nc, T, st):
    with ExitStack() as ctx:
        sb = lambda name, shape, dt=F32: ctx.enter_context(nc.sbuf_tensor(name, shape, dt))
        sem = lambda name: ctx.enter_context(nc.semaphore(name))
        cst, cols, modc, g1row, g2row, fgrow, cs, hT = (st[k] for k in (
            "cst", "cols", "modc", "g1row", "g2row", "fgrow", "cs", "hT"))
        prow = sb("prow", [P, P])
        ccol, csil = sb("ccol", [P, KD]), st["csil"]
        wada = sb("wada", [P, 2, KD * D])
        acc = sb("acc", [P, 2, D])
        posf, turns, posi = hT[:, 0], hT[:, 1], hT[:, 2].bitcast(I32)
        xt = sb("xt", [P, 2, GT, D])
        xsq = sb("xsq", [P, D])
        ss = sb("ss", [P, 2, GT])
        sr = sb("sr", [P, 2, GT])
        rx = sb("rx", [P, 2, GT])
        bank = ctx.enter_context(nc.psum_tensor("pbank", [P, 8, 512], F32))

        ld_small, ld_pos, ld_brow = sem("ld_small"), sem("ld_pos"), sem("ld_brow")
        ld_wada = [sem("ld_wada0"), sem("ld_wada1")]
        ld_x = [sem("ld_x0"), sem("ld_x1")]
        cols_turned, silu_done = sem("cols_turned"), sem("silu_done")
        angle_ready, sines_done = sem("angle_ready"), sem("sines_done")
        acc_ready, acc_used, mod_ready = sem("acc_ready"), sem("acc_used"), sem("mod_ready")
        squares_done, inverse_ready, scale_ready = sem("squares_done"), sem("inverse_ready"), sem("scale_ready")
        x_scaled, turned, h_even, h_odd = sem("x_scaled"), sem("turned"), sem("h_even"), sem("h_odd")
        dve_step = sem("dve_step0")
        block = ctx.enter_context(nc.Block())

        w_ada = T["w_ada"].rearrange("l (p k) n -> p (l k) n", k=KD)
        x_in = T["x"].rearrange("b (g q p) d -> p (b g) q d", p=P, q=GT)

        @block.sync
        def _(sp):
            small = [(cst[:], T["consts"][:, 0:C_SMALL]), (ccol[:], T["c"].rearrange("b (p k) -> p (b k)", k=KD)),
                     (prow[R_BADA:R_N1], rows(T["b_ada"])), (prow[R_N1:R_N2], rows(T["norm1_g"])),
                     (prow[R_N2:R_AO], rows(T["norm2_g"])), (prow[R_AO:R_CO], rows(T["attn_out_g"])),
                     (prow[R_CO:R_Q], rows(T["conv_out_g"])), (prow[R_Q:R_KV], rows(T["q_norm_g"])),
                     (prow[R_KV:R_CW], rows(T["kv_norm_g"])),
                     (prow[R_CW:R_CB], T["conv_w"].rearrange("l t (r c) -> (l t r) c", c=P)),
                     (prow[R_CB:R_ALL], rows(T["conv_b"]))]
            for dst, src in small:
                sp.dma_start(dst, src).then_inc(ld_small, 16)
            sp.dma_start(posi, T["positions"][0:1, :].partition_broadcast(P).rearrange("p a s -> p (a s)")
                         ).then_inc(ld_pos, 16)
            b = T["b_ada"]
            sp.dma_start(g1row[:], b[0, 2 * D:3 * D].partition_broadcast(P)).then_inc(ld_brow, 16)
            sp.dma_start(g2row[:], b[0, 5 * D:6 * D].partition_broadcast(P)).then_inc(ld_brow, 16)
            sp.dma_start(fgrow[:], T["final_g"].partition_broadcast(P)).then_inc(ld_brow, 16)
            for j in range(2):
                sp.dma_start(wada[:, j].rearrange("p (k n) -> p k n", k=KD),
                             w_ada[:, :, j * D:(j + 1) * D]).then_inc(ld_wada[j], 16)
            for g in range(2):
                sp.dma_start(xt[:, g], x_in[:, g]).then_inc(ld_x[g], 16)
            for g in range(2, NG):
                sp.wait_ge(turned, KD * (g - 1))
                sp.dma_start(xt[:, g % 2], x_in[:, g]).then_inc(ld_x[g % 2], 16)
            sp.wait_ge(ld_brow, 48)

        @block.vector
        def _(ve):
            V = Steps(ve, dve_step)
            ve.wait_ge(ld_small, 16 * 11)
            ve.wait_ge(ld_pos, 16)
            V(ve.tensor_copy(posf, posi))
            V.wait()
            V(ve.tensor_scalar(posf, posf, cst[:, C_FREQ:C_FREQ + 1], None, ALU.mult))
            V.wait()
            V(ve.tensor_scalar(turns, posf, 1 / TWO_PI, cst[:, C_TURN:C_TURN + 1], ALU.mult, ALU.add))
            V.wait()
            V(ve.tensor_scalar(turns, turns, ROUND, ROUND, ALU.add, ALU.subtract))
            for part in (PI_1, PI_2, PI_3, PI_4):
                V.wait()
                V(ve.scalar_tensor_tensor(posf, turns, -part, posf, ALU.mult, ALU.add))
            V.wait()
            V(ve.tensor_scalar(posf, posf, cst[:, C_PHASE:C_PHASE + 1], PI_IN, ALU.add, ALU.min))
            V.wait()
            V(ve.tensor_scalar(posf, posf, -PI_IN, None, ALU.max), angle_ready)
            ve.wait_ge(sines_done, 1)
            V(ve.tensor_scalar(cs[:], cs[:], cst[:, C_SIGN:C_SIGN + 1], None, ALU.mult))
            V.wait()
            V(ve.memset(cs[0:64, :], 1.0))
            ve.wait_ge(cols_turned, 1)
            V(ve.tensor_copy(cols[:, 0:R_ALL], bank[:, 0, 0:R_ALL]))
            ve.wait_ge(silu_done, 1)
            for j in range(2):
                a, w = acc[:, j % 2], wada[:, j % 2]
                ve.wait_ge(ld_wada[j], 16)
                V.wait()
                V(ve.tensor_scalar(a, w[:, 0:D], csil[:, 0:1], None, ALU.mult))
                for k in range(1, KD):
                    V.wait()
                    V(ve.scalar_tensor_tensor(a, w[:, k * D:(k + 1) * D], csil[:, k:k + 1], a, ALU.mult, ALU.add),
                      acc_ready if k == KD - 1 else None)
                if j == 1:
                    ve.wait_ge(acc_used, 2)
                    V(ve.tensor_tensor(modc[:, 0:16], bank[:, 1, 0:16], cols[:, 0:16], ALU.add))
                    V.wait()
                    V(ve.scalar_tensor_tensor(modc[:, 8:16], modc[:, 8:16], 1.0, cols[:, R_N1:R_N1 + 8],
                                              ALU.add, ALU.mult), mod_ready)
            V.wait()
            with ve.Fori(0, NG // 2) as gp:
                V.enter(gp, {dve_step: 2, inverse_ready: 2, x_scaled: 2 * GT, h_even: KD})
                for b in range(2):
                    ve.wait_ge(squares_done, gp * 2 * GT + b * GT + GT)
                    V.wait()
                    V(ve.tensor_scalar(sr[:, b], ss[:, b], 1 / D, EPS, ALU.mult, ALU.add))
                    V.wait()
                    V(ve.reciprocal(sr[:, b], sr[:, b]), inverse_ready)
                    ve.wait_ge(scale_ready, gp * 2 + b + 1)
                    for q in range(GT):
                        V(ve.tensor_scalar(xt[:, b, q], xt[:, b, q], rx[:, b, q:q + 1], None, ALU.mult), x_scaled)
                    for k in range(0, KD, 2):
                        ve.wait_ge(turned, gp * 2 * KD + b * KD + k + 1)
                        V(ve.tensor_scalar(hT[:, k, bass.ds(gp * 2 * GW + b * GW, GW)], bank[:, 4 + k % 4],
                                           modc[:, 8 + k:9 + k], modc[:, k:k + 1], ALU.mult, ALU.add), h_even)
                V.leave(NG // 2)

        @block.scalar
        def _(act):
            A = Steps(act, silu_done)
            act.wait_ge(ld_small, 16 * 11)
            A(act.activation(csil[:], ccol[:], ACT.Silu), silu_done)
            act.wait_ge(angle_ready, 1)
            A(act.activation(cs[:], posf, ACT.Sin), sines_done)
            A.wait()

            def squares(g):
                b = g % 2
                act.wait_ge(ld_x[b], 16 * (g // 2 + 1))
                for q in range(GT):
                    A.wait()
                    A(act.activation(xsq[:], xt[:, b, q], ACT.Square, accum_out=ss[:, b, q:q + 1]), squares_done)

            squares(0)
            act.wait_ge(mod_ready, 1)
            for g in range(NG):
                b = g % 2
                act.wait_ge(inverse_ready, g + 1)
                A(act.activation(rx[:, b], sr[:, b], ACT.Sqrt), scale_ready)
                if g + 1 < NG:
                    squares(g + 1)
                for k in range(1, KD, 2):
                    act.wait_ge(turned, g * KD + k + 1)
                    A(act.activation(hT[:, k, g * GW:(g + 1) * GW], bank[:, 4 + k % 4], ACT.Identity,
                                     scale=modc[:, 8 + k:9 + k], bias=modc[:, k:k + 1]), h_odd)

        @block.tensor
        def _(pe):
            pe.wait_ge(ld_small, 16 * 11)
            pe.transpose(bank[:, 0, 0:R_ALL], prow[0:R_ALL, :], cst[0:R_ALL, C_ID:C_ID + R_ALL]
                         ).then_inc(cols_turned, 1)
            for j in range(2):
                pe.wait_ge(acc_ready, j + 1)
                for k in range(KD):
                    ins = pe.matmul(bank[:, 1, j * KD + k:j * KD + k + 1], acc[:, j, k * P:(k + 1) * P],
                                    cst[:, C_ONE:C_ONE + 1], start=True, stop=True)
                ins.then_inc(acc_used, 1)
            with pe.Fori(0, NG // 2) as gp:
                for b in range(2):
                    pe.wait_ge(x_scaled, gp * 2 * GT + b * GT + GT)
                    for k in range(KD):
                        if k >= 4:
                            pe.wait_ge(h_odd if k % 2 else h_even, gp * KD + b * (KD // 2) + (k - 4) // 2 + 1)
                        elif b:
                            pe.wait_ge(h_odd if k % 2 else h_even, gp * KD + (k + 4) // 2 + 1)
                        else:
                            pe.wait_ge(h_odd if k % 2 else h_even, gp * KD)
                        for q in range(GT):
                            ins = pe.transpose(bank[:, 4 + k % 4, q * P:(q + 1) * P], xt[:, b, q, k * P:(k + 1) * P],
                                               cst[:, C_ID:C_ID + P])
                        ins.then_inc(turned, 1)


KR_COL = QR + KVR
U_COL = KR_COL + ROPE
B_COL = U_COL + CONV
C_COL = B_COL + CONV


LATE_HALVES = 4 * D // 512


def project(nc, T, st):
    with ExitStack() as ctx:
        sb = lambda name, shape, dt=F32: ctx.enter_context(nc.sbuf_tensor(name, shape, dt))
        sem = lambda name: ctx.enter_context(nc.semaphore(name))
        cst, cols, cs, hT, qn, kvn, KR, mix_dram = (st[k] for k in (
            "cst", "cols", "cs", "hT", "qn", "kvn", "KR", "mix_dram"))
        conv = sb("conv", [P, 2, S])
        wsl = sb("wsl", [P, 4, KD, P])
        wmod, macc, mterm = sb("wmod", [P, KD, 512]), sb("macc", [P, 512]), sb("mterm", [P, 512])
        csil, mod_dram = st["csil"], st["mod_dram"]
        t1, t2, t3, t4 = sb("t1", [P, S]), sb("t2", [P, S + TAPS - 1]), sb("t3", [P, S]), sb("t4", [P, S])
        bank = ctx.enter_context(nc.psum_tensor("abank", [P, 8, 512], F32))
        half = [bank[:, 0:4].rearrange("p a n -> p (a n)"), bank[:, 4:8].rearrange("p a n -> p (a n)")]

        ld_w = [sem(f"ld_w{i}") for i in range(4)]
        product_done, dve_read, u_copied = sem("product_done"), sem("dve_read"), sem("u_copied")
        squared, inverse_ready, scale_ready = sem("squared"), sem("inverse_ready1"), sem("scale_ready1")
        conv_stored = [sem("conv_stored0"), sem("conv_stored1")]
        dve_step = sem("dve_step1")
        ld_wmod, mod_step, mod_stored = sem("ld_wmod"), sem("mod_step"), sem("mod_stored")
        block = ctx.enter_context(nc.Block())
        w_in = T["w_in"].rearrange("l (k p) n -> p (l k) n", p=P)
        PAIRS = NCH // 2

        @block.sync
        def _(sp):
            for i in range(3):
                sp.dma_start(wsl[:, i], w_in[:, :, i * P:(i + 1) * P]).then_inc(ld_w[i], 16)
            h = ROPE // 2
            sp.dma_start(wsl[:, 3, :, 0:ROPE], w_in[:, :, KR_COL:KR_COL + ROPE]).then_inc(ld_w[3], 16)
            sp.dma_start(wsl[:, 3, :, ROPE:ROPE + h], w_in[:, :, KR_COL + h:KR_COL + ROPE]).then_inc(ld_w[3], 16)
            sp.dma_start(wsl[:, 3, :, ROPE + h:2 * ROPE], w_in[:, :, KR_COL:KR_COL + h]).then_inc(ld_w[3], 16)
            for i, col in enumerate((U_COL, C_COL, B_COL)):
                sp.wait_ge(product_done, i + 1)
                sp.dma_start(wsl[:, i], w_in[:, :, col:col + P]).then_inc(ld_w[i], 16)
            def store(ch, c):
                sp.wait_ge(dve_read, ch * 2 + 9)
                sp.dma_start(mix_dram[:, bass.ds(ch + NCH, 1)], conv[:, c:c + 1]).then_inc(conv_stored[c], 16)

            def weights(ch):
                for i, col in enumerate((U_COL, C_COL, B_COL)):
                    sp.wait_ge(product_done, 7 + ch * 3 - 3 + i + 1)
                    sp.dma_start(wsl[:, i], w_in[:, :, bass.ds(ch * P + col, P)]).then_inc(ld_w[i], 16)

            weights(1)
            with sp.Fori(1, PAIRS) as cp:
                for c in range(2):
                    weights(cp * 2 + c)
                    store(cp * 2 + (c - 2), c)
            store(NCH - 2, 0)
            store(NCH - 1, 1)
            for c in range(2):
                sp.wait_ge(conv_stored[c], 16 * PAIRS)

        @block.gpsimd
        def _(po):
            M = Steps(po, mod_step)
            w_ada = T["w_ada"].rearrange("l (p k) n -> p (l k) n", k=KD)
            for h in range(LATE_HALVES):
                at = 2 * D + h * 512
                M.wait()
                po.dma_start(wmod[:], w_ada[:, :, at:at + 512]).then_inc(ld_wmod, 16)
                po.wait_ge(ld_wmod, 16 * (h + 1))
                if h:
                    po.wait_ge(mod_stored, 16 * h)
                M(po.tensor_scalar(macc[:], wmod[:, 0], csil[:, 0:1], None, ALU.mult))
                for k in range(1, KD):
                    M.wait()
                    M(po.tensor_scalar(mterm[:], wmod[:, k], csil[:, k:k + 1], None, ALU.mult))
                    M.wait()
                    M(po.tensor_tensor(macc[:], macc[:], mterm[:], ALU.add))
                M.wait()
                po.dma_start(mod_dram[:, h], macc[:]).then_inc(mod_stored, 16)
            po.wait_ge(mod_stored, 16 * LATE_HALVES)

        @block.tensor
        def _(pe):
            ones = cst[:, C_ONE:C_ONE + P]

            def product(which, slot):
                for k in range(KD):
                    for n in range(4):
                        ins = pe.matmul(bank[:, 4 * which + n], wsl[:, slot, k], hT[:, k, n * 512:(n + 1) * 512],
                                        start=k == 0, stop=k == KD - 1)
                ins.then_inc(product_done, 1)

            def over_partitions(which, parts):
                for n in range(4):
                    for j, part in enumerate(parts):
                        ins = pe.matmul(bank[:, 4 * which + n], ones, part[:, n * 512:(n + 1) * 512],
                                        start=j == 0, stop=j == len(parts) - 1)
                ins.then_inc(product_done, 1)

            pe.wait_ge(ld_w[0], 16)
            product(0, 0)
            pe.wait_ge(ld_w[1], 16)
            product(1, 1)
            pe.wait_ge(ld_w[2], 16)
            pe.wait_ge(dve_read, 1)
            product(0, 2)
            pe.wait_ge(dve_read, 2)
            pe.wait_ge(squared, 2)
            over_partitions(1, (t1, t2))
            pe.wait_ge(ld_w[3], 48)
            pe.wait_ge(dve_read, 3)
            for k in range(KD):
                for n in range(4):
                    ins = pe.matmul(bank[64:128, n], wsl[:, 3, k, 0:64], hT[:, k, n * 512:(n + 1) * 512],
                                    start=k == 0, stop=k == KD - 1)
            ins.then_inc(product_done, 1)
            pe.wait_ge(dve_read, 4)
            pe.wait_ge(squared, 3)
            over_partitions(1, (t3,))
            pe.wait_ge(dve_read, 5)
            for n in range(4):
                ins = pe.matmul(bank[64:128, n], cst[64:128, C_FOLD:C_FOLD + 64], t4[64:128, n * 512:(n + 1) * 512],
                                start=True, stop=True)
            ins.then_inc(product_done, 1)
            with pe.Fori(0, PAIRS) as cp:
                for c in range(2):
                    for i in range(3):
                        pe.wait_ge(ld_w[i], cp * 32 + 16 * c + 32)
                        if i == 2:
                            pe.wait_ge(u_copied, cp * 2 + c + 1)
                        else:
                            pe.wait_ge(dve_read, cp * 4 + 2 * c + 6 + i)
                        product((1 + 3 * c + i) % 2, i)

        @block.vector
        def _(ve):
            V = Steps(ve, dve_step)

            def inverse(which, out, n, count):
                ve.wait_ge(product_done, count)
                V.wait()
                V(ve.tensor_scalar(out, half[which], 1 / n, EPS, ALU.mult, ALU.add), dve_read)
                V.wait()
                V(ve.reciprocal(out, out), inverse_ready)

            ve.wait_ge(product_done, 1)
            V(ve.tensor_copy(qn[:, 0], half[0]), dve_read)
            ve.wait_ge(product_done, 2)
            V(ve.tensor_copy(qn[:, 1], half[1]), dve_read)
            ve.wait_ge(product_done, 3)
            V(ve.tensor_copy(kvn[:], half[0]), dve_read)
            inverse(1, t1[:], QR, 4)
            ve.wait_ge(product_done, 5)
            V(ve.tensor_tensor(t4[64:128], half[0][64:128], cs[64:128], ALU.mult), dve_read)
            ve.wait_ge(scale_ready, 1)
            V(ve.tensor_tensor(qn[:, 0], qn[:, 0], t1[:], ALU.mult))
            V(ve.tensor_tensor(qn[:, 1], qn[:, 1], t1[:], ALU.mult))
            inverse(1, t3[:], KVR, 6)
            ve.wait_ge(product_done, 7)
            V(ve.tensor_copy(KR[64:128], half[0][64:128]), dve_read)
            ve.wait_ge(scale_ready, 2)
            V(ve.tensor_tensor(kvn[:], kvn[:], t3[:], ALU.mult))
            V(ve.memset(t2[:, 0:TAPS - 1], 0.0))
            V.wait()
            with ve.Fori(0, PAIRS) as cp:
                V.enter(cp, {dve_step: 2 * TAPS, dve_read: 4})
                for c in range(2):
                    tap = lambda i: cols[:, bass.ds(cp * 2 + (c + R_CW + i * NCH), 1)]
                    ve.wait_ge(product_done, cp * 6 + 3 * c + 7 + 2)
                    ve.wait_ge(u_copied, cp * 2 + c + 1)
                    V(ve.tensor_tensor(t2[:, TAPS - 1:], half[(1 + 3 * c + 1) % 2], t1[:], ALU.mult), dve_read)
                    V.wait()
                    V(ve.tensor_scalar(t3[:], t2[:, 2:], tap(2), cols[:, bass.ds(cp * 2 + (c + R_CB), 1)],
                                       ALU.mult, ALU.add))
                    for i in (1, 0):
                        V.wait()
                        V(ve.scalar_tensor_tensor(t3[:], t2[:, i:i + S], tap(i), t3[:], ALU.mult, ALU.add))
                    ve.wait_ge(product_done, cp * 6 + 3 * c + 7 + 3)
                    V.wait()
                    ve.wait_ge(conv_stored[c], cp * 16)
                    V(ve.tensor_tensor(conv[:, c], half[(1 + 3 * c + 2) % 2], t3[:], ALU.mult), dve_read)
                V.leave(PAIRS)

        @block.scalar
        def _(act):
            A = Steps(act, squared)
            act.wait_ge(dve_read, 1)
            A(act.activation(t1[:], qn[:, 0], ACT.Square), squared)
            act.wait_ge(dve_read, 2)
            A(act.activation(t2[:, 0:S], qn[:, 1], ACT.Square), squared)
            act.wait_ge(dve_read, 3)
            A(act.activation(t3[:], kvn[:], ACT.Square), squared)
            act.wait_ge(inverse_ready, 1)
            A(act.activation(t1[:], t1[:], ACT.Sqrt), scale_ready)
            act.wait_ge(inverse_ready, 2)
            A(act.activation(t3[:], t3[:], ACT.Sqrt), scale_ready)
            A.wait()
            with act.Fori(0, PAIRS) as cp:
                A.enter(cp, {u_copied: 2})
                for c in range(2):
                    act.wait_ge(product_done, cp * 6 + 3 * c + 7 + 1)
                    act.wait_ge(dve_read, cp * 4 + 2 * c + 7)
                    A.wait()
                    A(act.activation(t1[:], half[(1 + 3 * c) % 2], ACT.Copy), u_copied)
                A.leave(PAIRS)


GQ = 4
GROUPS = NT // GQ
STEP_OF = [(g, kt) for g in range(GROUPS) for kt in range(GQ * (g + 1))]
STEPS_HEAD = len(STEP_OF)
CHUNK_OF = [(i, n) for i in range(NT) for n in range(i // GQ + 1)]
assert len(CHUNK_OF) == STEPS_HEAD
AHEAD = 20
LEAD = 1
TILE_END = [CHUNK_OF.index((i, i // GQ)) for i in range(NT)]
SPREAD = [TILE_END[GQ * (g + 1) - 1] + 2 - AHEAD for g in range(GROUPS)]
SPREAD_AT = {m % STEPS_HEAD: (g, m < 0) for g, m in enumerate(SPREAD)}
MAXIMA_AHEAD = sum(c < AHEAD for c in TILE_END)
GROUPS_AHEAD = sum(m < 0 for m in SPREAD)
PART_AT = {2 + 3 * c: c for c in range(8)}
KEYS_AFTER, QUERIES_SPLIT_AFTER, QUERIES_REST_AFTER = 1, 2, 3
V_PARTS = NT // 4
V_AT = [(1, STEPS_HEAD - NT + 4 * (v + 1)) if v < V_PARTS - 1 else (0, 1) for v in range(V_PARTS)]
V_EARLY = V_PARTS - 1


def attend(nc, T, st):
    with ExitStack() as ctx:
        sb = lambda name, shape, dt=F32: ctx.enter_context(nc.sbuf_tensor(name, shape, dt))
        sem = lambda name: ctx.enter_context(nc.semaphore(name))
        cst, cols, cs, qn, kvn, KR, mix_dram = (st[k] for k in (
            "cst", "cols", "cs", "qn", "kvn", "KR", "mix_dram"))
        Qhi, Qlo = sb("Qhi", [P, 2, S], F32R), sb("Qlo", [P, 2, S], F32R)
        Khi, Klo = sb("Khi", [P, 2, S], F32R), sb("Klo", [P, 2, S], F32R)
        VV = sb("VV", [P, NT, 4, VD])
        probs = KR
        qf, turned_q = sb("qf", [P, 2, 512]), sb("turned_q", [P, 512])
        diag, onesr = sb("diag", [P, 2, 512], F32R), sb("onesr", [P, P], F32R)
        rs, on = sb("rs", [VD, 512]), sb("on", [VD, 2, 512])
        wuq = sb("wuq", [P, KQ, (HEADS + 1) * QKD])
        wuk, wuv = sb("wuk", [P, (HEADS + 1) * NOPE]), sb("wuv", [P, (HEADS + 2) * VD])
        wq, wk = sb("wq", [P, 2, KQ, P]), sb("wk", [P, 2, NOPE])
        cmax, nmax = sb("cmax", [P, 2, 4]), sb("nmax", [P, NT])
        bank = ctx.enter_context(nc.psum_tensor("tbank", [P, 8, 512], F32))
        scores, plain, outp, made, spread = bank[:, 0:2], bank[:, 2:4], bank[:, 4:6], bank[:, 6], bank[:, 7]

        ld_up = sem("ld_up")
        weights_ready, made_done, vmade_done, made_dve, v_copied = (sem(n) for n in (
            "weights_ready", "made_done", "vmade_done", "made_dve", "v_copied"))
        ld_rows, exp_done = sem("ld_rows"), sem("exp_done")
        khi_done, qf_ready, qhi_done, qlo_done = (sem(n) for n in ("khi_done", "qf_ready", "qhi_done", "qlo_done"))
        plain_done, plain_read, max_ready, diag_ready, spread_done, neg_copied = (sem(n) for n in (
            "plain_done", "plain_read", "max_ready", "diag_ready", "spread_done", "neg_copied"))
        scores_done, out_done, out_free = (sem(n) for n in ("scores_done", "out_done", "out_free"))
        stored = [sem("on_stored0"), sem("on_stored1")]
        dve_step, passed_pool = sem("dve_step2"), st["passed_pool"]
        block = ctx.enter_context(nc.Block())

        def key_cols(i, n):
            return min(512, (i + 1) * P - n * 512)

        def first_tile(g, kt):
            return max(kt - GQ * g, 0)

        def step_of(ap, m):
            if m == STEPS_HEAD - 1:
                return ap[:, 3 * 512:3 * 512 + P]
            return ap[:, m % 3 * 512 + first_tile(*STEP_OF[m]) * P:(m % 3 + 1) * 512]

        def chunk_at(m):
            return (m + AHEAD) % STEPS_HEAD, m + AHEAD >= STEPS_HEAD

        def maxima_before(m):
            return sum(chunk_at(k)[0] in TILE_END for k in range(m))

        @block.sync
        def _(sp):
            q = T["w_uq"].rearrange("l (k p) n -> p (l k) n", p=P)
            sp.dma_start(wuq[:, :, 0:HEADS * QKD], q).then_inc(ld_up, 16)
            sp.dma_start(wuq[:, :, HEADS * QKD:], q[:, :, 0:QKD]).then_inc(ld_up, 16)
            for w, name, more in ((wuk, "w_uk", 1), (wuv, "w_uv", 2)):
                src = T[name].rearrange("l p n -> p (l n)")
                sp.dma_start(w[:, 0:HEADS * NOPE], src).then_inc(ld_up, 16)
                sp.dma_start(w[:, HEADS * NOPE:], src[:, 0:more * NOPE]).then_inc(ld_up, 16)
            for k in range(2):
                sp.dma_start(qf[QKD:QKD + 1 + GQ, k], T["consts"][QKD:QKD + 1 + GQ, C_ROWS + k * 512:C_ROWS + (k + 1) * 512]
                             ).then_inc(ld_rows, 16)
            sp.sem_inc(stored[0], 16)
            with sp.Fori(0, HEADS // 2) as hp:
                for b in range(2):
                    for g in range(GROUPS):
                        sp.wait_ge(out_free, hp * 2 * GROUPS + (b * GROUPS + g + 2))
                        sp.dma_start(mix_dram[VD * b:VD * (b + 1), bass.ds(hp, 1), g * 512:(g + 1) * 512],
                                     on[:, (g + 1) % 2:(g + 1) % 2 + 1]).then_inc(stored[(g + 1) % 2], 16)
            sp.wait_ge(stored[0], 16 * (HEADS * GROUPS // 2 + 1))
            sp.wait_ge(stored[1], 16 * HEADS * GROUPS // 2)

        @block.tensor
        def _(pe):
            def make(c, b):
                n = c // 2
                if c % 2 == 0:
                    ins = pe.matmul(made[0:NOPE], wk[:, b], kvn[:, n * 512:(n + 1) * 512], start=True, stop=True)
                else:
                    for k in range(KQ):
                        ins = pe.matmul(made, wq[:, b, k], qn[:, k, n * 512:(n + 1) * 512],
                                        start=k == 0, stop=k == KQ - 1)
                ins.then_inc(made_done, 1)

            def make_values(v, pair):
                for j in range(4):
                    t = v * 4 + j
                    ins = pe.matmul(made[:, j * P:(j + 1) * P], kvn[:, t * P:(t + 1) * P],
                                    wuv[:, bass.ds(pair * 2 * VD, 2 * VD)], start=True, stop=True)
                ins.then_inc(vmade_done, 1)

            def plain_scores(chunk, b, seq):
                i, n = CHUNK_OF[chunk]
                w = key_cols(i, n)
                if not (isinstance(seq, int) and seq < 2):
                    pe.wait_ge(plain_read, seq - 1)
                pe.matmul(plain[:, chunk % 2, 0:w], Qhi[0:QKD, b, i * P:(i + 1) * P],
                          Khi[0:QKD, b, n * 512:n * 512 + w], start=True, stop=True).then_inc(plain_done, 1)

            def spread_maxima(g, head):
                pe.wait_ge(diag_ready, head * NT + GQ * (g + 1))
                if not (isinstance(head, int) and g == 0):
                    pe.wait_ge(neg_copied, head * GROUPS + g)
                pe.matmul(spread, onesr[:], diag[:, g % 2], start=True, stop=True).then_inc(spread_done, 1)

            pe.wait_ge(weights_ready, 1)
            for c in range(8):
                if c:
                    pe.wait_ge(made_dve, c)
                make(c, 0)
            pe.wait_ge(made_dve, 8)
            for v in range(V_EARLY):
                if v:
                    pe.wait_ge(v_copied, v)
                make_values(v, 0)
            pe.wait_ge(qlo_done, 4)
            for chunk in range(AHEAD):
                plain_scores(chunk, 0, chunk)
                if chunk - AHEAD in SPREAD:
                    spread_maxima(SPREAD.index(chunk - AHEAD), 0)

            def score(m, b, head):
                g, kt = STEP_OF[m]
                j = first_tile(g, kt)
                out = scores[:, m % 2, j * P:512]
                q = slice(g * 512 + j * P, (g + 1) * 512)
                k = slice(kt * P, (kt + 1) * P)
                if kt == 0:
                    pe.wait_ge(neg_copied, head * GROUPS + (g + 1))
                if not (isinstance(head, int) and m < 2):
                    pe.wait_ge(exp_done, head * STEPS_HEAD + (m - 1))
                every = QKD + 1 + (GQ if kt >= GQ * g else 0)
                pe.matmul(out, Khi[0:every, b, k], Qhi[0:every, b, q], start=True, stop=False)
                pe.matmul(out, Klo[0:QKD + 1, b, k], Qhi[0:QKD + 1, b, q], start=False, stop=False)
                pe.matmul(out, Khi[0:QKD + 1, b, k], Qlo[0:QKD + 1, b, q], start=False, stop=True
                          ).then_inc(scores_done, 1)

            for m in range(LEAD):
                score(m, 0, 0)
            with pe.Fori(0, HEADS // 2) as hp:
                for b in range(2):
                    head = hp * 2 + b
                    nxt = hp * 2 + (b + 1)

                    def value(m):
                        g, kt = STEP_OF[m]
                        pe.wait_ge(exp_done, hp * 2 * STEPS_HEAD + (b * STEPS_HEAD + m + 1))
                        if kt == 0:
                            pe.wait_ge(out_free, head * GROUPS + g)
                        if b == 0 and m == 0:
                            pe.wait_ge(v_copied, hp * V_PARTS + V_EARLY)
                        if b == 0 and (g, kt) == (GROUPS - 1, 4 * V_EARLY):
                            pe.wait_ge(v_copied, hp * V_PARTS + V_PARTS)
                        j = first_tile(g, kt)
                        out = outp[:, g % 2, j * P:512]
                        last = kt == GQ * (g + 1) - 1
                        ins = pe.matmul(out, VV[:, kt, 2 * b:2 * b + 2].rearrange("p c d -> p (c d)"),
                                        step_of(probs, m), start=kt == 0, stop=last)
                        if last:
                            ins.then_inc(out_done, 1)

                    for m in range(STEPS_HEAD):
                        if m + LEAD < STEPS_HEAD:
                            score(m + LEAD, b, head)
                        else:
                            score(m + LEAD - STEPS_HEAD, 1 - b, nxt)
                        chunk, ahead = chunk_at(m)
                        i, n = CHUNK_OF[chunk]
                        if i % GQ == 0 and n == 0:
                            pe.wait_ge(qlo_done, (nxt if ahead else head) * 4 + (i // GQ + 1))
                        plain_scores(chunk, 1 - b if ahead else b, hp * 2 * STEPS_HEAD + (b * STEPS_HEAD + AHEAD + m))
                        if m in PART_AT:
                            c = PART_AT[m]
                            if c == 0:
                                pe.wait_ge(weights_ready, nxt + 1)
                                if b == 0:
                                    pe.wait_ge(v_copied, hp * V_PARTS + V_PARTS)
                                else:
                                    pe.wait_ge(made_dve, nxt * 8)
                            else:
                                pe.wait_ge(made_dve, nxt * 8 + c)
                            make(c, 1 - b)
                        if (b, m) in V_AT:
                            v = V_AT.index((b, m))
                            if v == 0:
                                pe.wait_ge(made_dve, nxt * 8 + 8)
                            else:
                                pe.wait_ge(v_copied, hp * V_PARTS + (v if b == 0 else V_PARTS + v))
                            make_values(v, hp + b)
                        value(m)
                        if m in SPREAD_AT:
                            g, ahead = SPREAD_AT[m]
                            spread_maxima(g, nxt if ahead else head)

        @block.vector
        def _(ve):
            W = Steps(ve, dve_step)

            def weights(b, head):
                h = ROPE // 2
                at = head * QKD
                W(ve.tensor_copy(wq[:, b, :, 0:QKD], wuq[:, :, bass.ds(at, QKD)]))
                W(ve.tensor_copy(wq[:, b, :, QKD:QKD + h], wuq[:, :, bass.ds(at + (NOPE + h), h)]))
                W(ve.tensor_copy(wq[:, b, :, QKD + h:P], wuq[:, :, bass.ds(at + NOPE, h)]))
                W(ve.tensor_copy(wk[:, b], wuk[:, bass.ds(head * NOPE, NOPE)]), weights_ready)

            def part(c, b, head):
                n = c // 2
                at = slice(n * 512, (n + 1) * 512)
                if c % 2 == 0:
                    ve.wait_ge(khi_done, head * 4 + (n + 1))
                    W(ve.tensor_tensor(Klo[0:NOPE, b, at], made[0:NOPE], Khi[0:NOPE, b, at].bitcast(F32),
                                       ALU.subtract), made_dve)
                else:
                    ve.wait_ge(made_done, head * 8 + (c + 1))
                    ve.wait_ge(qlo_done, head * 4 + max(n - 1, 0))
                    W.wait()
                    W(ve.tensor_tensor(qf[0:QKD, n % 2], made[0:QKD], cs[0:QKD, at], ALU.mult))
                    W(ve.tensor_tensor(turned_q[NOPE:QKD], made[QKD:P], cs[QKD:P, at], ALU.mult), made_dve)
                    W.wait()
                    W(ve.tensor_tensor(qf[NOPE:QKD, n % 2], qf[NOPE:QKD, n % 2], turned_q[NOPE:QKD], ALU.add),
                      qf_ready)

            def maximum(chunk, seq):
                i, n = CHUNK_OF[chunk]
                last = chunk == TILE_END[i]
                w = key_cols(i, n)
                ve.wait_ge(plain_done, seq + 1)
                if last:
                    W(ve.memset(plain[0:64, chunk % 2, w - 64:w], -BIG))
                    W.wait()
                W(ve.tensor_reduce(cmax[:, i % 2, n:n + 1], plain[:, chunk % 2, 0:w], AX.X, ALU.max), plain_read)
                if last:
                    W.wait()
                    W(ve.tensor_reduce(nmax[:, i:i + 1], cmax[:, i % 2, 0:n + 1], AX.X, ALU.max, negate=True),
                      max_ready)

            def divide(r, g, head):
                if r == 0:
                    ve.wait_ge(out_done, head * GROUPS + (g + 1))
                    W.wait()
                W(ve.reciprocal(rs[:, r * P:(r + 1) * P], outp[VD:P, g % 2, r * P:(r + 1) * P]))
                if r == 3:
                    p = (g + 1) % 2
                    ve.wait_ge(stored[p], (head * 2 + (g + 1) // 2) * 16)
                    W.wait()
                    W(ve.tensor_tensor(on[:, p], outp[0:VD, g % 2], rs[:], ALU.mult), out_free)

            ve.wait_ge(ld_up, 16 * 6)
            for k in range(KQ):
                W(ve.tensor_scalar(wuq[:, k], wuq[:, k], cols[:, R_Q + k:R_Q + k + 1], SM, ALU.mult, ALU.mult))
            W(ve.tensor_scalar(wuk[:], wuk[:], cols[:, R_KV:R_KV + 1], None, ALU.mult))
            W(ve.tensor_scalar(wuv[:], wuv[:], cols[:, R_KV:R_KV + 1], None, ALU.mult))
            W.wait()
            weights(0, 0)
            W(ve.memset(VV[:, :, 1], 1.0))
            W(ve.memset(VV[:, :, 3], 1.0))
            W(ve.memset(outp[:, 1], 1.0))
            W(ve.tensor_copy(onesr[:], cst[:, C_ONE:C_ONE + P]))
            ve.wait_ge(ld_rows, 32)
            below = slice(QKD, QKD + 1 + GQ)
            one = cst[QKD:QKD + 1, C_ONE:C_ONE + 1].to_broadcast([1, S])
            for b in range(2):
                for k, parts in enumerate((Khi, Qhi)):
                    W(ve.tensor_copy(parts[below, b].rearrange("p (g n) -> p g n", g=GROUPS),
                                     qf[below, k].unsqueeze(1).to_broadcast([1 + GQ, GROUPS, 512])))
                W(ve.tensor_scalar(Klo[QKD:QKD + 1, b], one, 0.0, None, ALU.mult))
                W(ve.tensor_scalar(Qlo[QKD:QKD + 1, b], one, 0.0, None, ALU.mult))
                W(ve.tensor_copy(Khi[NOPE:QKD, b], KR[NOPE:QKD]))
                W.wait()
                W(ve.tensor_tensor(Klo[NOPE:QKD, b], KR[NOPE:QKD], Khi[NOPE:QKD, b].bitcast(F32), ALU.subtract))
            for c in range(8):
                part(c, 0, 0)
            W.wait()
            for chunk in range(AHEAD):
                maximum(chunk, chunk)
            W.wait()
            with ve.Fori(0, HEADS // 2) as hp:
                W.enter(hp, {dve_step: 2 * (3 + 4 + NT + GROUPS * 4), weights_ready: 2, made_dve: 16, qf_ready: 8,
                             plain_read: 2 * STEPS_HEAD, max_ready: 2 * NT, out_free: 2 * GROUPS})
                for b in range(2):
                    for m in range(STEPS_HEAD):
                        g, kt = STEP_OF[m]
                        maximum(chunk_at(m)[0], hp * 2 * STEPS_HEAD + (b * STEPS_HEAD + AHEAD + m))
                        if m == 0:
                            W.wait()
                            weights(1 - b, hp * 2 + (b + 1))
                        if PART_AT.get(m - KEYS_AFTER, 1) % 2 == 0:
                            part(PART_AT[m - KEYS_AFTER], 1 - b, hp * 2 + (b + 1))
                        if PART_AT.get(m, 0) % 2:
                            part(PART_AT[m], 1 - b, hp * 2 + (b + 1))
                        if kt < 4:
                            if g:
                                divide(kt, g - 1, hp * 2 + b)
                            else:
                                divide(kt, GROUPS - 1, hp * 2 + (b - 1))
                    if b == 0:
                        W.wait()
                W.leave(HEADS // 2)
            for r in range(4):
                divide(r, GROUPS - 1, HEADS - 1)

        @block.scalar
        def _(act):
            A = Steps(act, exp_done)

            def part(c, b, head):
                n = c // 2
                at = slice(n * 512, (n + 1) * 512)
                if c % 2 == 0:
                    act.wait_ge(made_done, head * 8 + (c + 1))
                    A(act.activation(Khi[0:NOPE, b, at], made[0:NOPE], ACT.Copy), khi_done)
                else:
                    act.wait_ge(qf_ready, head * 4 + (n + 1))
                    A(act.activation(Qhi[0:QKD, b, at], qf[0:QKD, n % 2], ACT.Copy), qhi_done)

            def copy_values(v, pair):
                act.wait_ge(vmade_done, pair * V_PARTS + (v + 1))
                A(act.activation(VV[:, v * 4:(v + 1) * 4, 0::2],
                                 made.rearrange("p (t c d) -> p t c d", c=2, d=VD), ACT.Copy), v_copied)

            def copy_maxima(g, b, head):
                act.wait_ge(spread_done, head * GROUPS + (g + 1))
                A(act.activation(Qhi[QKD:QKD + 1, b, g * 512:(g + 1) * 512], spread[QKD:QKD + 1], ACT.Copy),
                  neg_copied)

            for c in range(8):
                part(c, 0, 0)
            for v in range(V_EARLY):
                copy_values(v, 0)
            for g in range(GROUPS_AHEAD):
                copy_maxima(g, 0, 0)
            with act.Fori(0, HEADS // 2) as hp:
                for b in range(2):
                    for m in range(STEPS_HEAD):
                        g, kt = STEP_OF[m]
                        j = first_tile(g, kt)
                        act.wait_ge(scores_done, hp * 2 * STEPS_HEAD + (b * STEPS_HEAD + m + 1))
                        A(act.activation(step_of(probs, m), scores[:, m % 2, j * P:512], ACT.Exp), exp_done)
                        if PART_AT.get(m - KEYS_AFTER, 1) % 2 == 0:
                            part(PART_AT[m - KEYS_AFTER], 1 - b, hp * 2 + (b + 1))
                        if PART_AT.get(m - QUERIES_SPLIT_AFTER, 0) % 2:
                            part(PART_AT[m - QUERIES_SPLIT_AFTER], 1 - b, hp * 2 + (b + 1))
                        if (b, m - 1) in V_AT:
                            copy_values(V_AT.index((b, m - 1)), hp + b)
                        if m - 1 in SPREAD_AT:
                            g, ahead = SPREAD_AT[m - 1]
                            copy_maxima(g, 1 - b if ahead else b, hp * 2 + (b + ahead))

        @block.gpsimd
        def _(po):
            def rest(n, b, head):
                at = slice(n * 512, (n + 1) * 512)
                hold(po, qhi_done, head * 4 + (n + 1), passed_pool)
                po.tensor_tensor(Qlo[0:QKD, b, at], qf[0:QKD, n % 2], Qhi[0:QKD, b, at].bitcast(F32), ALU.subtract
                                 ).then_inc(qlo_done, 1)

            def diagonal(i, head):
                hold(po, max_ready, head * NT + (i + 1), passed_pool)
                po.tensor_scalar(diag[:, i // GQ % 2, i % GQ * P:(i % GQ + 1) * P], cst[:, C_ID:C_ID + P],
                                 nmax[:, i:i + 1], None, ALU.mult).then_inc(diag_ready, 1)

            for n in range(4):
                rest(n, 0, 0)
            for i in range(MAXIMA_AHEAD):
                diagonal(i, 0)
            with po.Fori(0, HEADS // 2) as hp:
                for b in range(2):
                    for m in range(STEPS_HEAD):
                        chunk, ahead = chunk_at(m)
                        if chunk in TILE_END:
                            diagonal(TILE_END.index(chunk), hp * 2 + (b + ahead))
                        if PART_AT.get(m - QUERIES_REST_AFTER, 0) % 2:
                            rest(PART_AT[m - QUERIES_REST_AFTER] // 2, 1 - b, hp * 2 + (b + 1))


def mix(nc, T, st):
    with ExitStack() as ctx:
        sb = lambda name, shape, dt=F32: ctx.enter_context(nc.sbuf_tensor(name, shape, dt))
        sem = lambda name: ctx.enter_context(nc.semaphore(name))
        cst, cols, modc, g1row, g2row, logits, mix_dram, mod_dram, x2_dram, xs_dram = (st[k] for k in (
            "cst", "cols", "modc", "g1row", "g2row", "logits", "mix_dram", "mod_dram", "x2_dram", "xs_dram"))
        macc = sb("macc_all", [P, LATE_HALVES, 512])
        NR = NGRP + NEXP
        wout = sb("wout", [P, 2 * NCH, D])
        whi, wlo = sb("whi", [P, 2 * NCH, D], F32R), sb("wlo", [P, 2 * NCH, D], F32R)
        mhi, mlo = sb("mhi", [P, 2, 2 * NCH, P], F32R), sb("mlo", [P, 2, 2 * NCH, P], F32R)
        wr, wrs = sb("wr", [P, KD, NR]), sb("wrs", [P, KD, NR])
        shift = sb("shift", [P, KD, P])
        rbias = sb("rbias", [P, NR])
        xin, mixed = sb("xin", [P, 2, D]), sb("mixed", [P, 2, 2 * NCH, P])
        sq, sqs = sb("sq", [P, 2 * NCH, P]), sb("sqs", [P, 2, P])
        junk = sb("junk", [P, D])
        x2, xs, xT = sb("x2", [P, 2, D]), sb("xs", [P, 2, D]), sb("xT", [P, 2, KD, P])
        mstat, xstat = sb("mstat", [P, 2, 2, 2]), sb("xstat", [P, 2, 3])
        bank = ctx.enter_context(nc.psum_tensor("mbank", [P, 8, 512], F32))
        sums, logit_bank, turn = bank[:, 0, 0:2], bank[:, 1, 0:NR], bank[:, 2:4]
        product = [bank[:, 4:6], bank[:, 6:8]]

        ld_wout, ld_r, ld_macc = [sem("ld_wout0"), sem("ld_wout1")], sem("ld_r"), sem("ld_macc")
        mod_summed, mod_read = sem("mod_summed"), sem("mod_read")
        ld_xin, ld_mixed = [sem("ld_xin0"), sem("ld_xin1")], [sem("ld_mixed0"), sem("ld_mixed1")]
        st_x2, st_xs = [sem("st_x20"), sem("st_x21")], [sem("st_xs0"), sem("st_xs1")]
        folded, whi_ready, wlo_even, wlo_odd = (
            sem(n) for n in ("folded", "whi_ready", "wlo_even", "wlo_odd"))
        shift_ready, rbias_done = sem("shift_ready"), sem("rbias_done")
        m_squared, m_reduced, m_summed, m_mean, m_inverse, m_scale = (sem(n) for n in (
            "m_squared", "m_reduced", "m_summed", "m_mean", "m_inverse", "m_scale"))
        mhi_ready, mlo_ready = sem("mhi_ready"), sem("mlo_ready")
        attn_done, conv_done, attn_added, x2_ready, x2_squared, x2_scale, xs_ready = (sem(n) for n in (
            "attn_done", "conv_done", "attn_added", "x2_ready", "x2_squared", "x2_scale", "xs_ready"))
        x2_step = sem("x2_step")
        x_turned, x_copied, routed, logit_ready = (sem(n) for n in ("x_turned", "x_copied", "routed", "logit_ready"))
        passed, passed_pool = st["passed"], st["passed_pool"]
        block = ctx.enter_context(nc.Block())
        x_rows = T["x"].rearrange("b s d -> (b s) d")

        def tiles(eng, step):
            step(0, 0)
            step(1, 1)
            with eng.Fori(0, (NT - 4) // 2) as i:
                for b in range(2):
                    step(i * 2 + (2 + b), b)
            step(NT - 2, 0)
            step(NT - 1, 1)

        def uses(t, b):
            return t // 2 * 16 if isinstance(t, int) else (t - b) * 8

        @block.sync
        def _(sp):
            sp.dma_start(macc[:], mod_dram).then_inc(ld_macc, 16)
            sp.dma_start(wr[:, :, 0:NGRP], T["w_router_group"].rearrange("l (k p) n -> p (l k) n", p=P)
                         ).then_inc(ld_r, 16)
            sp.dma_start(wr[:, :, NGRP:], T["w_router_expert"].rearrange("l (k p) n -> p (l k) n", p=P)
                         ).then_inc(ld_r, 16)
            sp.dma_start(rbias[:, 0:NGRP], T["b_router_group"][0, :].partition_broadcast(P)).then_inc(ld_r, 16)
            sp.dma_start(rbias[:, NGRP:], T["b_router_expert"][0, :].partition_broadcast(P)).then_inc(ld_r, 16)

            def load(t, b):
                sp.dma_start(mixed[:, b], mix_dram[:, :, bass.ds(t * P, P)]).then_inc(ld_mixed[b], 16)
                sp.dma_start(xin[:, b], x_rows[bass.ds(t * P, P), :]).then_inc(ld_xin[b], 16)

            def store(t, b):
                sp.wait_ge(x2_ready, t + 1)
                sp.dma_start(x2_dram[bass.ds(t * P, P), :], x2[:, b]).then_inc(st_x2[b], 16)
                sp.wait_ge(xs_ready, t + 1)
                sp.dma_start(xs_dram[bass.ds(t * P, P), :], xs[:, b]).then_inc(st_xs[b], 16)

            load(0, 0)
            w_out = T["w_out"].rearrange("l (k p) n -> p (l k) n", p=P)
            for h in range(2):
                sp.dma_start(wout[:, h * NCH:(h + 1) * NCH], w_out[:, h * NCH:(h + 1) * NCH]).then_inc(ld_wout[h], 16)
            load(1, 1)
            with sp.Fori(0, (NT - 2) // 2) as i:
                for b in range(2):
                    sp.wait_ge(attn_added, i * 2 + (b + 1))
                    sp.wait_ge(conv_done, i * 2 + (b + 1))
                    load(i * 2 + (2 + b), b)
                    store(i * 2 + b, b)
            store(NT - 2, 0)
            store(NT - 1, 1)
            for b in range(2):
                sp.wait_ge(st_x2[b], 16 * NT // 2)
                sp.wait_ge(st_xs[b], 16 * NT // 2)

        @block.tensor
        def _(pe):
            ident = cst[:, C_ID:C_ID + P]

            def part(h, b, done):
                for k in range(h * NCH, (h + 1) * NCH):
                    for j, (m, w) in enumerate(((mhi, whi), (mlo, whi), (mhi, wlo))):
                        for n in range(2):
                            ins = pe.matmul(product[h][:, n], m[:, b, k], w[:, k, n * 512:(n + 1) * 512],
                                            start=k == h * NCH and j == 0, stop=k == (h + 1) * NCH - 1 and j == 2)
                ins.then_inc(done, 1)

            def sum_squares(t, b):
                pe.wait_ge(m_reduced, t + 1)
                pe.wait_ge(m_mean, t)
                for h in range(2):
                    ins = pe.matmul(sums[:, h:h + 1], sqs[:, h], cst[:, C_ONE:C_ONE + 1], start=True, stop=True)
                ins.then_inc(m_summed, 1)

            def turn_x(t, b):
                pe.wait_ge(xs_ready, t + 1)
                pe.wait_ge(x_copied, t)
                for k in range(KD):
                    ins = pe.transpose(turn[:, k // 4, (k % 4) * P:(k % 4 + 1) * P], xs[:, b, k * P:(k + 1) * P],
                                       ident)
                ins.then_inc(x_turned, 1)

            def route(t, b):
                pe.wait_ge(x_copied, t + 1)
                pe.wait_ge(logit_ready, t)
                for k in range(KD):
                    ins = pe.matmul(logit_bank, xT[:, b, k], wrs[:, k], start=k == 0, stop=k == KD - 1)
                ins.then_inc(routed, 1)

            def step(t, b):
                pe.wait_ge(mhi_ready, t + 1)
                pe.wait_ge(mlo_ready, t + 1)
                pe.wait_ge(attn_added, t)
                first = isinstance(t, int) and t == 0
                if first:
                    pe.wait_ge(wlo_even, NCH // 2)
                    pe.wait_ge(wlo_odd, NCH // 2)
                part(0, b, attn_done)
                if not isinstance(t, int) or t < NT - 1:
                    sum_squares(t + 1, 1 - b)
                if not isinstance(t, int) or t >= 2:
                    route(t - 2, b)
                pe.wait_ge(x2_ready, t)
                if first:
                    pe.wait_ge(wlo_even, NCH)
                    pe.wait_ge(wlo_odd, NCH)
                part(1, b, conv_done)
                if not isinstance(t, int) or t >= 1:
                    turn_x(t - 1, 1 - b)

            pe.wait_ge(ld_macc, 16)
            for n in range(2):
                ins = pe.matmul(product[0][:, n], cst[:, C_ONE:C_ONE + P], macc[:, n], start=True, stop=True)
            ins.then_inc(mod_summed, 1)
            for k in range(2 * KD):
                ins = pe.matmul(turn[:, 0, k:k + 1], macc[:, 2 + k // 4, k % 4 * P:(k % 4 + 1) * P],
                                cst[:, C_ONE:C_ONE + 1], start=True, stop=True)
            ins.then_inc(mod_summed, 1)
            for n in range(2):
                ins = pe.matmul(product[1][:, n], cst[:, C_ONE:C_ONE + P], macc[:, 6 + n], start=True, stop=True)
            ins.then_inc(mod_summed, 1)
            pe.wait_ge(shift_ready, 1)
            for k in range(KD):
                ins = pe.matmul(logit_bank, shift[:, k], wr[:, k], start=k == 0, stop=k == KD - 1)
            ins.then_inc(rbias_done, 1)
            sum_squares(0, 0)
            pe.wait_ge(mod_read, 4)
            tiles(pe, step)
            route(NT - 2, 0)
            turn_x(NT - 1, 1)
            route(NT - 1, 1)

        @block.vector
        def _(ve):
            def reduce_squares(t, b):
                ve.wait_ge(m_squared, t + 1)
                ve.wait_ge(m_summed, t)
                ve.tensor_reduce(sqs[:].unsqueeze(3), sq[:].rearrange("p (h k) n -> p h n k", h=2), AX.X, ALU.add
                                 ).then_inc(m_reduced, 1)

            def mixers_scale(t, b):
                ve.wait_ge(m_summed, t + 1)
                ve.tensor_scalar(mstat[:, b, 0], sums, 1 / ATTN, EPS, ALU.mult, ALU.add).then_inc(m_mean, 1)
                ve.wait_ge(m_mean, t + 1)
                ve.reciprocal(mstat[:, b, 0], mstat[:, b, 0]).then_inc(m_inverse, 1)

            def add_attention(t, b):
                ve.wait_ge(attn_done, t + 1)
                ve.wait_ge(m_scale, t + 1)
                ve.wait_ge(ld_xin[b], uses(t, b) + 16)
                ve.wait_ge(st_x2[b], uses(t, b))
                ve.scalar_tensor_tensor(x2[:, b], product[0].rearrange("p a n -> p (a n)"), mstat[:, b, 1, 0:1],
                                        xin[:, b], ALU.mult, ALU.add).then_inc(attn_added, 1)

            def add_conv(t, b):
                ve.wait_ge(conv_done, t + 1)
                ve.wait_ge(attn_added, t + 1)
                ve.scalar_tensor_tensor(x2[:, b], product[1].rearrange("p a n -> p (a n)"), mstat[:, b, 1, 1:2],
                                        x2[:, b], ALU.mult, ALU.add).then_inc(x2_ready, 1)
                ve.wait_ge(x2_squared, t + 1)
                ve.tensor_scalar(xstat[:, b, 1:2], xstat[:, b, 0:1], 1 / D, EPS, ALU.mult, ALU.add
                                 ).then_inc(x2_step, 1)
                ve.wait_ge(x2_step, t * 2 + 1)
                ve.reciprocal(xstat[:, b, 1:2], xstat[:, b, 1:2]).then_inc(x2_step, 1)
                ve.wait_ge(x2_scale, t + 1)
                ve.wait_ge(st_xs[b], uses(t, b))
                ve.tensor_scalar(xs[:, b], x2[:, b], xstat[:, b, 2:3], None, ALU.mult).then_inc(xs_ready, 1)

            def logit(t, b):
                ve.wait_ge(routed, t + 1)
                out = logits[:, t] if isinstance(t, int) else logits[:, bass.ds(t, 1)].rearrange("p a n -> p (a n)")
                ve.tensor_tensor(out, logit_bank, rbias[:], ALU.add).then_inc(logit_ready, 1)

            def step(t, b):
                last = isinstance(t, int) and t == NT - 1
                if not last:
                    reduce_squares(t + 1, 1 - b)
                add_attention(t, b)
                if not last:
                    mixers_scale(t + 1, 1 - b)
                if not isinstance(t, int) or t >= 2:
                    logit(t - 2, b)
                add_conv(t, b)

            ve.wait_ge(mod_summed, 1)
            ve.tensor_tensor(g1row[:], g1row[:], product[0].rearrange("p a n -> p (a n)"), ALU.add
                             ).then_inc(mod_read, 1)
            ve.wait_ge(mod_summed, 2)
            ve.tensor_tensor(modc[:, 16:32], turn[:, 0, 0:16], cols[:, 24:40], ALU.add).then_inc(mod_read, 1)
            ve.wait_ge(mod_read, 2)
            ve.scalar_tensor_tensor(modc[:, 24:32], modc[:, 24:32], 1.0, cols[:, R_N2:R_N2 + 8], ALU.add, ALU.mult
                                    ).then_inc(mod_read, 1)
            ve.wait_ge(mod_summed, 3)
            ve.tensor_tensor(g2row[:], g2row[:], product[1].rearrange("p a n -> p (a n)"), ALU.add
                             ).then_inc(mod_read, 1)
            ve.wait_ge(mod_read, 4)
            ve.wait_ge(ld_r, 16 * 4)
            for k in range(KD):
                ve.tensor_scalar(wrs[:, k], wr[:, k], modc[:, 24 + k:25 + k], None, ALU.mult)
                ins = ve.tensor_scalar(shift[:, k], cst[:, C_ONE:C_ONE + P], modc[:, 16 + k:17 + k], None, ALU.mult)
            ins.then_inc(shift_ready, 1)
            reduce_squares(0, 0)
            ve.wait_ge(rbias_done, 1)
            ve.tensor_tensor(rbias[:], logit_bank, rbias[:], ALU.add)
            mixers_scale(0, 0)
            for k in range(2 * NCH + 1):
                if k < 2 * NCH:
                    ve.wait_ge(ld_wout[k // NCH], 16)
                    gain = cols[:, R_AO + k:R_AO + k + 1]
                    ve.scalar_tensor_tensor(wout[:, k], wout[:, k], gain, g1row[:], ALU.mult, ALU.mult
                                            ).then_inc(folded, 1)
                if k % 2:
                    ve.wait_ge(whi_ready, k)
                    ve.tensor_tensor(wlo[:, k - 1], wout[:, k - 1], whi[:, k - 1].bitcast(F32), ALU.subtract
                                     ).then_inc(wlo_even, 1)
            tiles(ve, step)
            logit(NT - 2, 0)
            logit(NT - 1, 1)

        @block.scalar
        def _(act):
            def mixers_in(t, b):
                hold(act, ld_mixed[b], uses(t, b) + 16, passed)
                hold(act, conv_done, t - 1 if not isinstance(t, int) or t >= 2 else 0, passed)
                act.activation(mhi[:, b], mixed[:, b], ACT.Copy).then_inc(mhi_ready, 1)
                act.wait_ge(m_reduced, t)
                act.activation(sq[:], mixed[:, b], ACT.Square).then_inc(m_squared, 1)

            def mixers_scale(t, b):
                act.wait_ge(m_inverse, t + 1)
                act.activation(mstat[:, b, 1], mstat[:, b, 0], ACT.Sqrt).then_inc(m_scale, 1)

            def copy_x(t, b):
                act.wait_ge(x_turned, t + 1)
                act.activation(xT[:, b].rearrange("p k n -> p (k n)"), turn.rearrange("p a n -> p (a n)"), ACT.Copy
                               ).then_inc(x_copied, 1)

            def step(t, b):
                last = isinstance(t, int) and t == NT - 1
                if not last:
                    mixers_in(t + 1, 1 - b)
                    mixers_scale(t + 1, 1 - b)
                act.wait_ge(x2_ready, t + 1)
                act.activation(junk[:], x2[:, b], ACT.Square, accum_out=xstat[:, b, 0:1]).then_inc(x2_squared, 1)
                act.wait_ge(x2_step, t * 2 + 2)
                act.activation(xstat[:, b, 2:3], xstat[:, b, 1:2], ACT.Sqrt).then_inc(x2_scale, 1)
                if not isinstance(t, int) or t >= 1:
                    copy_x(t - 1, 1 - b)

            mixers_in(0, 0)
            for k in range(2 * NCH):
                act.wait_ge(folded, k + 1)
                act.activation(whi[:, k], wout[:, k], ACT.Copy).then_inc(whi_ready, 1)
            mixers_scale(0, 0)
            tiles(act, step)
            copy_x(NT - 1, 1)

        @block.gpsimd
        def _(po):
            def step(t, b):
                hold(po, mhi_ready, t + 1, passed_pool)
                po.tensor_tensor(mlo[:, b], mixed[:, b], mhi[:, b].bitcast(F32), ALU.subtract
                                 ).then_inc(mlo_ready, 1)

            step(0, 0)
            for k in range(1, 2 * NCH, 2):
                po.wait_ge(whi_ready, k + 1)
                po.tensor_tensor(wlo[:, k], wout[:, k], whi[:, k].bitcast(F32), ALU.subtract).then_inc(wlo_odd, 1)
            step(1, 1)
            with po.Fori(0, (NT - 2) // 2) as i:
                for b in range(2):
                    step(i * 2 + (2 + b), b)


def route(nc, T, st):
    with ExitStack() as ctx:
        sb = lambda name, shape, dt=F32: ctx.enter_context(nc.sbuf_tensor(name, shape, dt))
        sem = lambda name: ctx.enter_context(nc.semaphore(name))
        cst, logits, gates, rank, marks, rounds = (st[k] for k in (
            "cst", "logits", "gates", "rank", "marks", "rounds"))
        g1, gexp, gcand, gone, gpen = (sb(n, [P, NT, NGRP]) for n in ("g1", "gexp", "gcand", "gone", "gpen"))
        best, pgrp, low = sb("best", [P, 2, NT, 1]), sb("pgrp", [P, NT, 1]), sb("low", [P, NT, 1])
        em, cand = sb("em", [P, NT, NEXP]), sb("cand", [P, NT, NEXP])
        pick = sb("pick", [P, NT, 2, NEXP])
        tmp = sb("tmp", [P, NT, 2, NEXP])
        both = sb("both", [P, NT * NEXP], BF16)
        trib, oneb = sb("trib", [P, P], BF16), sb("oneb", [P, P], BF16)
        dexp = sb("dexp", [P, NT, 1])
        most, need, need1 = sb("most", [P, 1]), sb("need", [P, ROUNDS]), sb("need1", [P, 1])
        bank = ctx.enter_context(nc.psum_tensor("rbank", [P, 2, 512], F32))
        dve_step, less_best, group_exp, pair_less, pair_exp = (sem(n) for n in (
            "dve_step4", "less_best", "group_exp", "pair_less", "pair_exp"))
        both_ready, ranked = sem("both_ready"), sem("ranked")
        block = ctx.enter_context(nc.Block())

        def across(ap, n, k):
            return ap.to_broadcast([P, n, k])

        def repeat(ap, n):
            return ap.unsqueeze(1).to_broadcast([P, n, ap.shape[-1]])

        @block.vector
        def _(ve):
            V = Steps(ve, dve_step)

            def do(ins, sem=None):
                V(ins, sem)
                V.wait()

            G, E = logits[:, :, 0:NGRP], logits[:, :, NGRP:]
            top = best[:, 0]
            do(ve.tensor_copy(trib[:], cst[:, C_TRI:C_TRI + P]))
            do(ve.tensor_copy(oneb[:], cst[:, C_ONE:C_ONE + P]))
            do(ve.tensor_reduce(top, G, AX.X, ALU.max))
            do(ve.tensor_tensor(g1[:], G, across(top, NT, NGRP), ALU.subtract), less_best)
            do(ve.tensor_tensor(gone[:], G, across(top, NT, NGRP), ALU.is_equal))
            do(ve.scalar_tensor_tensor(gcand[:], gone[:], -64.0, repeat(cst[:, C_GRP:C_GRP + NGRP], NT),
                                       ALU.mult, ALU.add))
            do(ve.tensor_reduce(low[:], gcand[:], AX.X, ALU.min))
            do(ve.tensor_tensor(gone[:], gcand[:], across(low[:], NT, NGRP), ALU.is_equal))
            do(ve.tensor_scalar(gpen[:], gone[:], BIG, BIG, ALU.mult, ALU.subtract))
            ve.wait_ge(group_exp, 1)
            do(ve.tensor_reduce(pgrp[:], gexp[:], AX.X, ALU.add))
            do(ve.reciprocal(pgrp[:], pgrp[:]))
            in_groups = lambda ap: ap.rearrange("p t (g e) -> p t g e", g=NGRP)
            on_experts = lambda ap: ap.unsqueeze(3).to_broadcast([P, NT, NGRP, EPG])
            do(ve.tensor_tensor(in_groups(em[:]), in_groups(E), on_experts(gone[:]), ALU.mult))
            do(ve.tensor_tensor(in_groups(em[:]), in_groups(em[:]), on_experts(gpen[:]), ALU.add))
            for k in range(2):
                m = best[:, k]
                do(ve.tensor_reduce(m, em[:], AX.X, ALU.max))
                do(ve.tensor_tensor(cand[:], em[:], across(m, NT, NEXP), ALU.is_equal))
                do(ve.scalar_tensor_tensor(cand[:], cand[:], -64.0, repeat(cst[:, C_EXP:C_EXP + NEXP], NT),
                                           ALU.mult, ALU.add))
                do(ve.tensor_reduce(low[:], cand[:], AX.X, ALU.min))
                do(ve.tensor_tensor(pick[:, :, k], cand[:], across(low[:], NT, NEXP), ALU.is_equal))
                if k == 0:
                    do(ve.scalar_tensor_tensor(em[:], pick[:, :, 0], -3 * BIG, em[:], ALU.mult, ALU.add))
            do(ve.tensor_tensor(both[:].rearrange("p (t e) -> p t e", t=NT), pick[:, :, 0], pick[:, :, 1], ALU.add),
               both_ready)
            do(ve.tensor_tensor(dexp[:], best[:, 1], best[:, 0], ALU.subtract), pair_less)
            ve.wait_ge(pair_exp, 1)
            do(ve.tensor_scalar(low[:], dexp[:], 1.0, None, ALU.add))
            do(ve.reciprocal(low[:], low[:]))
            do(ve.tensor_tensor(gates[:, 0::2].unsqueeze(2), low[:], pgrp[:], ALU.mult))
            do(ve.tensor_tensor(gates[:, 1::2].unsqueeze(2), gates[:, 0::2].unsqueeze(2), dexp[:], ALU.mult))
            for k in range(2):
                do(ve.tensor_tensor(marks[:, :, k, 0:NEXP], pick[:, :, k],
                                    cst[:, C_SLOT:C_SLOT + NT].unsqueeze(2).to_broadcast([P, NT, NEXP]), ALU.mult))
                do(ve.tensor_scalar(marks[:, :, k, 2 * NEXP:], pick[:, :, k], float(1 + k), None, ALU.mult))
                do(ve.tensor_scalar(marks[:, :, k, NEXP:2 * NEXP], pick[:, :, k], cst[:, C_PART:C_PART + 1], None, ALU.mult))
            ve.wait_ge(ranked, 1)
            before = bank[:, 0].rearrange("p (t e) -> p t e", t=NT)
            for k in range(2):
                do(ve.tensor_tensor(tmp[:, :, k], pick[:, :, k], before, ALU.mult))
            do(ve.tensor_reduce(rank[:].rearrange("p (t k) -> p t k", k=2), tmp[:], AX.X, ALU.add))
            do(ve.tensor_reduce(most[:], bank[:, 1, 0:NEXP], AX.X, ALU.max))
            do(ve.tensor_scalar(need[:], cst[:, C_RND:C_RND + ROUNDS], most[:], None, ALU.is_lt))
            do(ve.tensor_reduce(need1[:], need[:], AX.X, ALU.add))
            do(ve.tensor_copy(rounds[:], need1[:]))

        @block.scalar
        def _(act):
            act.wait_ge(less_best, 1)
            act.activation(gexp[:], g1[:], ACT.Exp).then_inc(group_exp, 1)
            act.wait_ge(pair_less, 1)
            act.activation(dexp[:], dexp[:], ACT.Exp).then_inc(pair_exp, 1)

        @block.tensor
        def _(pe):
            pe.wait_ge(both_ready, 1)
            pe.matmul(bank[:, 0], trib[:], both[:], start=True, stop=False)
            for j in range(1, NT):
                pe.matmul(bank[:, 0, j * NEXP:], oneb[:], both[:, 0:(NT - j) * NEXP], start=False, stop=j == NT - 1)
            for t in range(NT):
                ins = pe.matmul(bank[:, 1, 0:NEXP], oneb[:], both[:, t * NEXP:(t + 1) * NEXP],
                                start=t == 0, stop=t == NT - 1)
            ins.then_inc(ranked, 1)


def experts(nc, T, st):
    with ExitStack() as ctx:
        sb = lambda name, shape, dt=F32: ctx.enter_context(nc.sbuf_tensor(name, shape, dt))
        sem = lambda name: ctx.enter_context(nc.semaphore(name))
        cst, modc, rank, marks, rounds, xs_dram, y_dram = (st[k] for k in (
            "cst", "modc", "rank", "marks", "rounds", "xs_dram", "y_dram"))
        inslot = sb("inslot", [P, NT * 2, CAP], BF16)
        slot_a, slot_b = sb("slot_a", [P, NEXP + 1], I32), sb("slot_b", [CAPB, NEXP + 1], I32)
        dest_a, dest_b = sb("dest_a", [P, NEXP], I32), sb("dest_b", [CAPB, NEXP], I32)
        tab_a, tab_b = sb("tab_a", [P, 3 * NEXP]), sb("tab_b", [CAPB, 3 * NEXP])
        dump_b, row_a, row_b = sb("dump_b", [CAPB, NEXP]), sb("row_a", [P, NEXP]), sb("row_b", [CAPB, NEXP])
        ia, ib = sb("ia", [P, 2], I32), sb("ib", [CAPB, 2], I32)
        ja, jb = sb("ja", [P, 2], I32), sb("jb", [CAPB, 2], I32)
        xa, xb = sb("xa", [P, 2, D]), sb("xb", [CAPB, 2, D])
        xT = sb("xTe", [P, 2, KD, CAP])
        wg, wu, wd = sb("wg", [P, 2, KD, FE]), sb("wu", [P, 2, KD, FE]), sb("wd", [P, 2, KF, D])
        sg, aT = sb("sg", [P, KF, CAP]), sb("aT", [P, KF, CAP])
        dhi, dlo = sb("dhi", [P, KF, D], F32R), sb("dlo", [P, KF, D], F32R)
        ahi, alo = sb("ahi", [P, KF, CAP], F32R), sb("alo", [P, KF, CAP], F32R)
        ya, yb = sb("ya", [P, 2, D]), sb("yb", [CAPB, 2, D])
        bank = ctx.enter_context(nc.psum_tensor("ebank", [P, 8, 512], F32))
        turn, gate, up, outa, outb = bank[:, 0:2], bank[:, 2], bank[:, 3], bank[:, 4:6], bank[0:CAPB, 6:8]

        slots_ready, table_summed, table_ready = sem("slots_ready"), sem("table_summed"), sem("table_ready")
        idx_copied, dest_copied = sem("idx_copied"), sem("dest_copied")
        gathered, turned = [sem("gathered0"), sem("gathered1")], [sem("xturned0"), sem("xturned1")]
        ld_exp = [sem("ld_exp0"), sem("ld_exp1")]
        turn_dve, turn_act = sem("turn_dve"), sem("turn_act")
        gate_done, up_done, silu_done = sem("gate_done"), sem("up_done"), sem("silu_done5")
        mlp_step = sem("mlp_step")
        down_a, down_b, ya_done, yb_done = sem("down_a"), sem("down_b"), sem("ya_done"), sem("yb_done")
        st_ya, st_yb = [sem("st_ya0"), sem("st_ya1")], [sem("st_yb0"), sem("st_yb1")]
        dhi_ready, dlo_ready = sem("dhi_ready"), sem("dlo_ready")
        dve_step, dump_ready = sem("dve_step5"), sem("dump_ready")
        passed, passed_pool = st["passed"], st["passed_pool"]
        block = ctx.enter_context(nc.Block())
        PAIRS = NEXP // 2
        TURNS = NEXP + 1

        def load_rounds(eng):
            return eng.value_load(rounds[0:1, 0:1], min_val=1, max_val=ROUNDS)

        @block.sync
        def _(sp):
            n_rounds = load_rounds(sp)
            wgd = T["w_exp_gate"].rearrange("l e (k p) n -> p (l e k) n", p=P)
            wud = T["w_exp_up"].rearrange("l e (k p) n -> p (l e k) n", p=P)
            wdd = T["w_exp_down"].rearrange("l e (k p) n -> p (l e k) n", p=P)
            with sp.Fori(0, n_rounds) as r:
                with sp.Fori(0, PAIRS) as ep:
                    for b in range(2):
                        sp.wait_ge(down_b, r * NEXP + ep * 2 + (b + 1))
                        sp.dma_start(wg[:, b], wgd[:, bass.ds(ep * 2 * KD + b * KD, KD), :]).then_inc(ld_exp[b], 16)
                        sp.dma_start(wu[:, b], wud[:, bass.ds(ep * 2 * KD + b * KD, KD), :]).then_inc(ld_exp[b], 16)
                        sp.dma_start(wd[:, b], wdd[:, bass.ds(ep * 2 * KF + b * KF, KF), :]).then_inc(ld_exp[b], 16)

        @block.gpsimd
        def _(po):
            n_rounds = load_rounds(po)

            def gather(b, column, use, copied):
                hold(po, turned[b], use * 4, passed_pool)
                po.tensor_copy(ia[:, b:b + 1], slot_a[:, bass.ds(column, 1)]).then_inc(idx_copied, 1)
                po.tensor_copy(ib[:, b:b + 1], slot_b[:, bass.ds(column, 1)]).then_inc(idx_copied, 1)
                hold(po, idx_copied, copied * 2 + 2, passed_pool)
                for x, i in ((xa, ia), (xb, ib)):
                    po.indirect_dma_start(out=x[:, b], out_offset=None, in_=xs_dram,
                                          in_offset=bass.IndirectOffsetOnAxis(ap=i[:, b:b + 1], axis=0)
                                          ).then_inc(gathered[b], 16)

            def scatter(b, column, use, e):
                hold(po, st_ya[b], use * 16, passed_pool)
                hold(po, st_yb[b], use * 16, passed_pool)
                po.tensor_copy(ja[:, b:b + 1], dest_a[:, bass.ds(column, 1)]).then_inc(dest_copied, 1)
                po.tensor_copy(jb[:, b:b + 1], dest_b[:, bass.ds(column, 1)]).then_inc(dest_copied, 1)
                hold(po, dest_copied, e * 2 + 2, passed_pool)
                for y, j, done, stored in ((ya, ja, ya_done, st_ya), (yb, jb, yb_done, st_yb)):
                    hold(po, done, e + 1, passed_pool)
                    po.indirect_dma_start(out=y_dram, in_=y[:, b], in_offset=None,
                                          out_offset=bass.IndirectOffsetOnAxis(ap=j[:, b:b + 1], axis=0)
                                          ).then_inc(stored[b], 16)

            with po.Fori(0, n_rounds) as r:
                hold(po, table_ready, r * 6 + 6, passed_pool)
                gather(0, r * 0, r * (PAIRS + 1), r * TURNS)
                gather(1, r * 0 + 1, r * PAIRS, r * TURNS + 1)
                with po.Fori(0, PAIRS - 1) as ep:
                    for b in range(2):
                        gather(b, ep * 2 + (2 + b), r * (PAIRS + 1 - b) + ep + 1, r * TURNS + ep * 2 + (2 + b))
                        scatter(b, ep * 2 + b, r * PAIRS + ep, r * NEXP + ep * 2 + b)
                gather(0, r * 0 + NEXP, r * (PAIRS + 1) + PAIRS, r * TURNS + NEXP)
                for b in range(2):
                    scatter(b, r * 0 + (NEXP - 2 + b), r * PAIRS + (PAIRS - 1), r * NEXP + (NEXP - 2 + b))
            for b in range(2):
                hold(po, st_ya[b], n_rounds * (PAIRS * 16), passed_pool)
                hold(po, st_yb[b], n_rounds * (PAIRS * 16), passed_pool)

        @block.tensor
        def _(pe):
            n_rounds = load_rounds(pe)
            ident = cst[:, C_ID:C_ID + P]

            def turn_in(b, groups, use, seq):
                for g in groups:
                    if g == 0:
                        pe.wait_ge(gathered[b], use * 32 + 32)
                    pe.wait_ge(turn_act if g % 2 else turn_dve, seq * 4 + g // 2 * 2)
                    for j in range(2):
                        k = 2 * g + j
                        pe.transpose(turn[:, g % 2, j * CAP:j * CAP + P], xa[:, b, k * P:(k + 1) * P], ident)
                        ins = pe.transpose(turn[:, g % 2, j * CAP + P:(j + 1) * CAP], xb[:, b, k * P:(k + 1) * P],
                                           cst[0:CAPB, C_ID:C_ID + CAPB])
                    ins.then_inc(turned[b], 1)

            def down(out, lo, hi, done):
                for f in range(KF):
                    for j, (a, w) in enumerate(((ahi, dhi), (alo, dhi), (ahi, dlo))):
                        for n in range(2):
                            ins = pe.matmul(out[:, n], a[:, f, lo:hi], w[:, f, n * 512:(n + 1) * 512],
                                            start=f == 0 and j == 0, stop=f == KF - 1 and j == 2)
                ins.then_inc(done, 1)

            pe.sem_inc(down_b, 2)
            with pe.Fori(0, n_rounds) as r:
                pe.wait_ge(slots_ready, r + 1)
                pe.wait_ge(ya_done, r * NEXP)
                for out, lo, n in ((bank[:, 4, 0:3 * NEXP], 0, P), (bank[0:CAPB, 5, 0:3 * NEXP], P, CAPB)):
                    for j in range(NT * 2):
                        ins = pe.matmul(out, inslot[:, j, lo:lo + n],
                                        marks[:, j // 2, j % 2], start=j == 0, stop=j == NT * 2 - 1)
                    ins.then_inc(table_summed, 1)
                turn_in(0, range(4), r * (PAIRS + 1), r * TURNS)
                with pe.Fori(0, PAIRS) as ep:
                    for b in range(2):
                        e = r * NEXP + ep * 2 + b
                        seq = r * TURNS + ep * 2 + b
                        pe.wait_ge(ld_exp[b], r * (PAIRS * 48) + ep * 48 + 48)
                        pe.wait_ge(turn_dve, seq * 4 + 4)
                        pe.wait_ge(turn_act, seq * 4 + 4)
                        for w, out, done in ((wg, gate, gate_done), (wu, up, up_done)):
                            for f in range(KF):
                                for k in range(KD):
                                    ins = pe.matmul(out[:, f * CAP:(f + 1) * CAP], w[:, b, k, f * P:(f + 1) * P],
                                                    xT[:, b, k], start=k == 0, stop=k == KD - 1)
                            ins.then_inc(done, 1)
                        nxt = (1 - b, r * (PAIRS + b) + ep + b, seq + 1)
                        turn_in(nxt[0], (0, 1), nxt[1], nxt[2])
                        pe.wait_ge(mlp_step, e * 3 + 3)
                        pe.wait_ge(dlo_ready, e + 1)
                        pe.wait_ge(ya_done, e)
                        down(outa, 0, P, down_a)
                        turn_in(nxt[0], (2, 3), nxt[1], nxt[2])
                        pe.wait_ge(yb_done, e)
                        down(outb, P, CAP, down_b)

        @block.vector
        def _(ve):
            n_rounds = load_rounds(ve)

            def copy_in(b, groups, use):
                for g in groups:
                    ve.wait_ge(turned[b], use * 4 + g + 1)
                    for j in range(2):
                        k = 2 * g + j
                        ve.tensor_scalar(xT[:, b, k], turn[:, 0, j * CAP:(j + 1) * CAP], modc[:, 24 + k:25 + k],
                                         modc[:, 16 + k:17 + k], ALU.mult, ALU.add).then_inc(turn_dve, 1)

            ve.tensor_scalar(dump_b[:], cst[0:CAPB, C_DUMP:C_DUMP + NEXP], float(P), None, ALU.add
                             ).then_inc(dump_ready, 1)
            with ve.Fori(0, n_rounds) as r:
                ve.wait_ge(table_summed, r * 2)
                ve.wait_ge(dve_step, r * 9)
                ve.tensor_tensor(inslot[:], cst[:, C_SLOT:C_SLOT + CAP].unsqueeze(1).to_broadcast([P, NT * 2, CAP]),
                                 rank[:].unsqueeze(2).to_broadcast([P, NT * 2, CAP]), ALU.is_equal
                                 ).then_inc(slots_ready, 1)
                ve.wait_ge(slots_ready, r + 1)
                ve.tensor_scalar(rank[:], rank[:], float(-CAP), None, ALU.add).then_inc(dve_step, 1)
                ve.wait_ge(idx_copied, r * (TURNS * 2))
                ve.wait_ge(dest_copied, r * (NEXP * 2))
                ve.wait_ge(dump_ready, 1)
                for j, (psum, tab, dump, row, slot, dest) in enumerate((
                        (bank[:, 4], tab_a, cst[:, C_DUMP:C_DUMP + NEXP], row_a, slot_a, dest_a),
                        (bank[0:CAPB, 5], tab_b, dump_b[:], row_b, slot_b, dest_b))):
                    tile, in_tile, mark = (tab[:, n * NEXP:(n + 1) * NEXP] for n in range(3))
                    ve.wait_ge(table_summed, r * 2 + (j + 1))
                    ve.wait_ge(dve_step, r * 9 + (4 * j + 1))
                    ve.tensor_copy(tab[:], psum[:, 0:3 * NEXP]).then_inc(dve_step, 1)
                    ve.wait_ge(dve_step, r * 9 + (4 * j + 2))
                    ve.scalar_tensor_tensor(slot[:, 0:NEXP], tile, float(P), in_tile, ALU.mult, ALU.add
                                            ).then_inc(table_ready, 1)
                    ve.scalar_tensor_tensor(row[:], mark, 0.0, dump, ALU.is_equal, ALU.mult).then_inc(dve_step, 1)
                    ve.wait_ge(dve_step, r * 9 + (4 * j + 3))
                    ve.tensor_tensor(row[:], row[:], mark, ALU.add).then_inc(dve_step, 1)
                    ve.wait_ge(dve_step, r * 9 + (4 * j + 4))
                    ve.scalar_tensor_tensor(row[:], in_tile, 2.0, row[:], ALU.mult, ALU.add).then_inc(dve_step, 1)
                    ve.wait_ge(dve_step, r * 9 + (4 * j + 5))
                    ve.scalar_tensor_tensor(dest[:], tile, 2.0 * P, row[:], ALU.mult, ALU.add
                                            ).then_inc(table_ready, 1)
                ve.wait_ge(table_ready, r * 6 + 4)
                ve.tensor_copy(slot_a[:, NEXP:], slot_a[:, 0:1]).then_inc(table_ready, 1)
                ve.tensor_copy(slot_b[:, NEXP:], slot_b[:, 0:1]).then_inc(table_ready, 1)
                copy_in(0, (0, 2), r * (PAIRS + 1))
                with ve.Fori(0, PAIRS) as ep:
                    for b in range(2):
                        e = r * NEXP + ep * 2 + b
                        ve.wait_ge(dhi_ready, e + 1)
                        ve.tensor_tensor(dlo[:], wd[:, b], dhi[:].bitcast(F32), ALU.subtract).then_inc(dlo_ready, 1)
                        ve.wait_ge(up_done, e + 1)
                        ve.wait_ge(silu_done, e + 1)
                        ve.tensor_tensor(aT[:].rearrange("p f n -> p (f n)"), sg[:].rearrange("p f n -> p (f n)"),
                                         up[:, 0:KF * CAP], ALU.mult).then_inc(mlp_step, 1)
                        ve.wait_ge(mlp_step, e * 3 + 1)
                        ve.tensor_copy(ahi[:], aT[:]).then_inc(mlp_step, 1)
                        ve.wait_ge(mlp_step, e * 3 + 2)
                        ve.tensor_tensor(alo[:], aT[:], ahi[:].bitcast(F32), ALU.subtract).then_inc(mlp_step, 1)
                        copy_in(1 - b, (0, 2), r * (PAIRS + b) + ep + b)
                        ve.wait_ge(down_b, e + 3)
                        ve.wait_ge(st_yb[b], r * (PAIRS * 16) + ep * 16)
                        ve.tensor_copy(yb[:, b], outb.rearrange("p a n -> p (a n)")).then_inc(yb_done, 1)

        @block.scalar
        def _(act):
            n_rounds = load_rounds(act)

            def copy_in(b, groups, use):
                for g in groups:
                    act.wait_ge(turned[b], use * 4 + g + 1)
                    for j in range(2):
                        k = 2 * g + j
                        act.activation(xT[:, b, k], turn[:, 1, j * CAP:(j + 1) * CAP], ACT.Identity,
                                       scale=modc[:, 24 + k:25 + k], bias=modc[:, 16 + k:17 + k]
                                       ).then_inc(turn_act, 1)

            with act.Fori(0, n_rounds) as r:
                copy_in(0, (1, 3), r * (PAIRS + 1))
                with act.Fori(0, PAIRS) as ep:
                    for b in range(2):
                        e = r * NEXP + ep * 2 + b
                        use = r * (PAIRS + b) + ep + b
                        act.wait_ge(down_b, e + 2)
                        hold(act, ld_exp[b], r * (PAIRS * 48) + ep * 48 + 48, passed)
                        act.activation(dhi[:], wd[:, b], ACT.Copy).then_inc(dhi_ready, 1)
                        act.wait_ge(gate_done, e + 1)
                        act.activation(sg[:].rearrange("p f n -> p (f n)"), gate[:, 0:KF * CAP], ACT.Silu
                                       ).then_inc(silu_done, 1)
                        copy_in(1 - b, (1,), use)
                        act.wait_ge(down_a, e + 1)
                        act.wait_ge(st_ya[b], r * (PAIRS * 16) + ep * 16)
                        act.activation(ya[:, b], outa.rearrange("p a n -> p (a n)"), ACT.Copy).then_inc(ya_done, 1)
                        copy_in(1 - b, (3,), use)


def combine(nc, T, st, out):
    with ExitStack() as ctx:
        sb = lambda name, shape, dt=F32: ctx.enter_context(nc.sbuf_tensor(name, shape, dt))
        sem = lambda name: ctx.enter_context(nc.semaphore(name))
        g2row, fgrow, gates, x2_dram, y_dram = (st[k] for k in ("g2row", "fgrow", "gates", "x2_dram", "y_dram"))
        NB = 4
        y, x2, res = sb("y", [P, NB, 2, D]), sb("x2f", [P, NB, D]), sb("res", [P, 2, D])
        junk = sb("junkf", [P, D])
        stat = sb("statf", [P, NB, 3])
        ld = [sem(f"ld_y_x2_{b}") for b in range(NB)]
        st_out = [sem(f"st_out{b}") for b in range(2)]
        first_gated, summed, gated, added = (sem(n) for n in ("first_gated", "y_summed", "y_gated", "added"))
        squared, scale, normed = sem("squared6"), sem("scale6"), sem("normed")
        stat_step = sem("stat_step6")
        passed = st["passed"]
        block = ctx.enter_context(nc.Block())
        out_rows = out.rearrange("b s d -> (b s) d")
        pairs = y_dram[1:1 + 2 * S, :].rearrange("(t k) d -> t k d", k=2)

        def tiles(eng, step):
            for b in range(NB):
                step(0, b)
            with eng.Fori(1, NT // NB) as i:
                for b in range(NB):
                    step(i, b)

        @block.sync
        def _(sp):
            def load(t, b):
                sp.dma_start(y[:, b], pairs[bass.ds(t * P, P)]).then_inc(ld[b], 16)
                sp.dma_start(x2[:, b], x2_dram[bass.ds(t * P, P), :]).then_inc(ld[b], 16)

            def store(t, b):
                sp.wait_ge(normed, t + 1)
                sp.dma_start(out_rows[bass.ds(t * P, P), :], res[:, b % 2]).then_inc(st_out[b % 2], 16)

            for b in range(NB):
                load(b, b)
            with sp.Fori(0, NT // NB - 1) as i:
                for b in range(NB):
                    store(i * NB + b, b)
                    load(i * NB + (b + NB), b)
            for b in range(NB):
                store(NT - NB + b, b)
            for b in range(2):
                sp.wait_ge(st_out[b], 16 * NT // 2)

        @block.scalar
        def _(act):
            def root(i, b):
                act.wait_ge(stat_step, i * (2 * NB) + (2 * b + 2))
                act.activation(stat[:, b, 2:3], stat[:, b, 1:2], ACT.Sqrt).then_inc(scale, 1)

            def step(i, b):
                hold(act, ld[b], i * 32 + 32, passed)
                act.activation(y[:, b, 0], y[:, b, 0], ACT.Copy, scale=gates[:, bass.ds(i * (2 * NB) + 2 * b, 1)]
                               ).then_inc(first_gated, 1)
                if b:
                    root(i, b - 1)
                elif not isinstance(i, int):
                    root(i - 1, NB - 1)
                act.wait_ge(added, i * NB + (b + 1))
                act.activation(junk[:], x2[:, b], ACT.Square, accum_out=stat[:, b, 0:1]).then_inc(squared, 1)

            tiles(act, step)
            root(NT // NB - 1, NB - 1)

        @block.vector
        def _(ve):
            def mean(i, b):
                ve.wait_ge(squared, i * NB + (b + 1))
                ve.tensor_scalar(stat[:, b, 1:2], stat[:, b, 0:1], 1 / D, EPS, ALU.mult, ALU.add
                                 ).then_inc(stat_step, 1)
                ve.wait_ge(stat_step, i * (2 * NB) + (2 * b + 1))
                ve.reciprocal(stat[:, b, 1:2], stat[:, b, 1:2]).then_inc(stat_step, 1)

            def norm(i, b):
                ve.wait_ge(scale, i * NB + (b + 1))
                ve.wait_ge(st_out[b % 2], i * (8 * NB) + b // 2 * 16)
                ve.scalar_tensor_tensor(res[:, b % 2], x2[:, b], stat[:, b, 2:3], fgrow[:], ALU.mult, ALU.mult
                                        ).then_inc(normed, 1)

            def step(i, b):
                n = i * NB + (b + 1)
                before = (i, b - 1) if b else None if isinstance(i, int) else (i - 1, NB - 1)
                ve.wait_ge(first_gated, n)
                ve.scalar_tensor_tensor(y[:, b, 1], y[:, b, 1], gates[:, bass.ds(i * (2 * NB) + (2 * b + 1), 1)],
                                        y[:, b, 0], ALU.mult, ALU.add).then_inc(summed, 1)
                if before:
                    mean(*before)
                ve.wait_ge(summed, n)
                ve.tensor_tensor(y[:, b, 0], y[:, b, 1], g2row[:], ALU.mult).then_inc(gated, 1)
                ve.wait_ge(gated, n)
                ve.tensor_tensor(x2[:, b], x2[:, b], y[:, b, 0], ALU.add).then_inc(added, 1)
                if before:
                    norm(*before)

            tiles(ve, step)
            mean(NT // NB - 1, NB - 1)
            norm(NT // NB - 1, NB - 1)


def program(nc, T, out):
    with ExitStack() as whole:
        def tensor(scope, side=None):
            return lambda name, shape, dt=F32: scope.enter_context(nc.sbuf_tensor(name, shape, dt, side=side))

        keep = tensor(whole)
        scratch = lambda name, shape: nc.dram_tensor(name, shape, F32, kind="Internal").ap()
        st = {"cst": keep("cst", [P, C_SMALL]), "cols": keep("cols", [P, 96]), "modc": keep("modcol", [P, 32]),
              "csil": keep("csil", [P, KD]),
              "mod_dram": scratch("mod_dram", [P, LATE_HALVES, 512]), "g1row": keep("g1row", [P, D]), "g2row": keep("g2row", [P, D]), "fgrow": keep("fgrow", [P, D]),
              "mix_dram": scratch("mix_dram", [P, 2 * NCH, S]), "x2_dram": scratch("x2_dram", [S, D]),
              "xs_dram": scratch("xs_dram", [S, D]), "y_dram": scratch("y_dram", [1 + 2 * S + 2 * CAP, D])}
        st["passed"], st["passed_pool"] = (whole.enter_context(nc.semaphore(n)) for n in ("passed", "passed_pool"))
        with ExitStack() as mixers:
            left = tensor(mixers)
            st["cs"] = left("cs", [P, S])
            with ExitStack() as first:
                st["hT"] = tensor(first, "right")("hT", [P, KD, S])
                prepare(nc, T, st)
                st["qn"], st["kvn"], st["KR"] = left("qn", [P, KQ, S]), left("kvn", [P, S]), left("KR", [P, S])
                project(nc, T, st)
            attend(nc, T, st)
        st["logits"] = keep("logits", [P, NT, NGRP + NEXP])
        mix(nc, T, st)
        st["gates"], st["rank"] = keep("gates", [P, NT * 2]), keep("rank", [P, NT * 2])
        st["marks"], st["rounds"] = keep("marks", [P, NT, 2, 3 * NEXP], BF16), keep("rounds", [P, 1], I32)
        route(nc, T, st)
        experts(nc, T, st)
        combine(nc, T, st, out)


_INS = ["x", "c", "positions", "w_ada", "b_ada", "norm1_g", "w_in", "q_norm_g", "kv_norm_g", "w_uq", "w_uk", "w_uv",
        "conv_w", "conv_b", "attn_out_g", "conv_out_g", "w_out", "norm2_g", "w_router_group", "b_router_group",
        "w_router_expert", "b_router_expert", "w_exp_gate", "w_exp_up", "w_exp_down", "final_g"]


def kernel(**inputs):
    import concourse.bacc as bacc
    from concourse.bass_utils import run_bass_kernel_spmd

    nc = bacc.Bacc("TRN2", target_bir_lowering=False, num_devices=1)
    arrays = {f"in_{n}": np.ascontiguousarray(inputs[n]) for n in _INS}
    arrays["in_consts"] = constants()
    T = {n[3:]: nc.dram_tensor(n, a.shape, mybir.dt.from_np(a.dtype), kind="ExternalInput").ap()
         for n, a in arrays.items()}
    out = nc.dram_tensor("out", [1, S, D], F32, kind="ExternalOutput").ap()
    program(nc, T, out)
    r = run_bass_kernel_spmd(nc, [arrays], core_ids=[0])
    return r.results[0]["out"]
```
